# Optimizing a Trainium2 kernel written in Bass

```python
import jax, jax.numpy as jnp
from jax import lax
import numpy as np

D_MODEL = 1024
BATCH = 1
SEQ = 256
DEPTH = 2

N_GROUPS = 4
FOURIER_WIDTH = 512
FOURIER_GROUP = FOURIER_WIDTH // N_GROUPS
CONV_WIDTH = 512
CONV_K = 3
POOL_WIDTH = 512
POOL_GROUP = POOL_WIDTH // N_GROUPS
POOL_WINDOWS = (2, 4, 8, 16)
OUT_GROUP = D_MODEL // N_GROUPS
N_BRANCHES = 3
D_FF = 2816
EPS = 1e-6

OFF_F = 0
OFF_B = OFF_F + FOURIER_WIDTH
OFF_C = OFF_B + CONV_WIDTH
OFF_V = OFF_C + CONV_WIDTH
OFF_P = OFF_V + CONV_WIDTH
OFF_G = OFF_P + POOL_WIDTH
IN_WIDTH = OFF_G + N_BRANCHES * D_MODEL


def rmsnorm(x, g):
    xf = x.astype(jnp.float32)
    y = xf * lax.rsqrt(jnp.mean(xf * xf, axis=-1, keepdims=True) + EPS)
    return (y * g.astype(jnp.float32)).astype(x.dtype)

def swiglu(h, w1, w3, w2):
    return (jax.nn.silu(h @ w1) * (h @ w3)) @ w2

def fourier_mix(u, w_map):
    b, s, _ = u.shape
    ug = u.reshape(b, s, N_GROUPS, FOURIER_GROUP).astype(jnp.float32)
    f = jnp.fft.fftn(ug, axes=(1, 3), norm="ortho").real.astype(u.dtype)
    y = jnp.einsum("bsgc,gcd->bsgd", f, w_map)
    return y.reshape(b, s, D_MODEL)

def short_conv(bg, cg, v, w_conv, w_out):
    z = cg * v
    zp = jnp.pad(z, ((0, 0), (1, 1), (0, 0)))
    conv = w_conv[0] * zp[:, :-2] + w_conv[1] * zp[:, 1:-1] + w_conv[2] * zp[:, 2:]
    return (bg * conv) @ w_out

def pool_mix(u, w_map, scale):
    s = u.shape[1]
    t = jnp.arange(s, dtype=jnp.float32)
    outs = []
    for i, w in enumerate(POOL_WINDOWS):
        half = w // 2
        ug = u[..., i * POOL_GROUP:(i + 1) * POOL_GROUP].astype(jnp.float32)
        cs = jnp.pad(jnp.cumsum(ug, axis=1), ((0, 0), (1, 0), (0, 0)))
        padded = jnp.pad(cs, ((0, 0), (half, half), (0, 0)), mode="edge")
        win = padded[:, w:w + s] - padded[:, :s]
        count = jnp.minimum(t + half, float(s)) - jnp.maximum(t - half, 0.0)
        pooled = win / count[None, :, None] - ug
        outs.append(pooled.astype(u.dtype) @ w_map[i])
    return jnp.concatenate(outs, axis=-1) * scale

def first_inputs(seed: int = 0) -> dict:
    key = jax.random.key(seed)
    ks = jax.random.split(key, 20)
    f32 = jnp.float32

    def nrm(k, shape, fan_in):
        return jax.random.normal(k, shape, f32) * (fan_in ** -0.5)

    def gain(k, shape):
        return 1.0 + 0.02 * jax.random.normal(k, shape, f32)

    L, D = DEPTH, D_MODEL
    return {
        "x": jax.random.normal(ks[0], (BATCH, SEQ, D), f32),
        "g_ffn1": gain(ks[1], (L, D)),
        "w1_a": nrm(ks[2], (L, D, D_FF), D),
        "w3_a": nrm(ks[3], (L, D, D_FF), D),
        "w2_a": nrm(ks[4], (L, D_FF, D), D_FF),
        "g_mix": gain(ks[5], (L, D)),
        "w_in": nrm(ks[6], (L, D, IN_WIDTH), D),
        "w_fourier": nrm(ks[7], (L, N_GROUPS, FOURIER_GROUP, OUT_GROUP), FOURIER_GROUP),
        "w_conv": nrm(ks[8], (L, CONV_K, CONV_WIDTH), CONV_K),
        "w_conv_out": nrm(ks[9], (L, CONV_WIDTH, D), CONV_WIDTH),
        "w_pool": nrm(ks[10], (L, N_GROUPS, POOL_GROUP, OUT_GROUP), POOL_GROUP),
        "pool_scale": gain(ks[11], (L, D)),
        "w_o": nrm(ks[12], (L, D, D), D),
        "g_ffn2": gain(ks[13], (L, D)),
        "w1_b": nrm(ks[14], (L, D, D_FF), D),
        "w3_b": nrm(ks[15], (L, D, D_FF), D),
        "w2_b": nrm(ks[16], (L, D_FF, D), D_FF),
        "g_final": gain(ks[17], (D,)),
    }

def first_block(x, g_ffn1, w1_a, w3_a, w2_a, g_mix, w_in, w_fourier, w_conv, w_conv_out,
              w_pool, pool_scale, w_o, g_ffn2, w1_b, w3_b, w2_b, g_final):
    b, s, d = x.shape
    for l in range(DEPTH):
        h = rmsnorm(x, g_ffn1[l])
        x = x + 0.5 * swiglu(h, w1_a[l], w3_a[l], w2_a[l])

        h = rmsnorm(x, g_mix[l])
        p = h @ w_in[l]
        gates = jax.nn.sigmoid(p[..., OFF_G:].astype(jnp.float32)).astype(x.dtype)
        gates = gates.reshape(b, s, N_BRANCHES, d)
        y_f = fourier_mix(p[..., OFF_F:OFF_B], w_fourier[l])
        y_c = short_conv(p[..., OFF_B:OFF_C], p[..., OFF_C:OFF_V], p[..., OFF_V:OFF_P],
                         w_conv[l], w_conv_out[l])
        y_p = pool_mix(p[..., OFF_P:OFF_G], w_pool[l], pool_scale[l])
        merged = gates[:, :, 0] * y_f + gates[:, :, 1] * y_c + gates[:, :, 2] * y_p
        x = x + merged @ w_o[l]

        h = rmsnorm(x, g_ffn2[l])
        x = x + 0.5 * swiglu(h, w1_b[l], w3_b[l], w2_b[l])
    return rmsnorm(x, g_final)


SWA_HEADS = 8
SWA_KV_HEADS = 2
SWA_HEAD_DIM = 64
SWA_WINDOW = 128
SWA_BLOCK = 128
ROPE_THETA = 10000.0
GLA_HEADS = 4
GLA_DK = D_MODEL // 2 // GLA_HEADS
GLA_DV = D_MODEL // GLA_HEADS
GLA_GATE_RANK = 16
GLA_TAU = 16.0
GLA_CHUNK = 64

SWA_Q_W = SWA_HEADS * SWA_HEAD_DIM
SWA_KV_W = SWA_KV_HEADS * SWA_HEAD_DIM
GLA_K_W = GLA_HEADS * GLA_DK
GLA_V_W = GLA_HEADS * GLA_DV
IN_SPLITS = (SWA_Q_W, SWA_KV_W, SWA_KV_W, GLA_K_W, GLA_K_W, GLA_V_W, GLA_V_W, GLA_GATE_RANK, D_MODEL, D_MODEL)
IN_COLS = sum(IN_SPLITS)


def rmsnorm_2(x, g):
    xf = x.astype(jnp.float32)
    y = xf * lax.rsqrt(jnp.mean(xf * xf, axis=-1, keepdims=True) + EPS)
    return (y * g.astype(jnp.float32)).astype(x.dtype)

def swiglu_2(h, w_gate, w_up, w_down):
    return (jax.nn.silu(h @ w_gate) * (h @ w_up)) @ w_down

def split_cols(z, sizes):
    idx = np.cumsum(np.array(sizes))[:-1].tolist()
    return jnp.split(z, idx, axis=-1)

def rope_tables(T):
    inv_freq = ROPE_THETA ** (-jnp.arange(0, SWA_HEAD_DIM, 2, dtype=jnp.float32) / SWA_HEAD_DIM)
    ang = jnp.arange(T, dtype=jnp.float32)[:, None] * inv_freq[None, :]
    return jnp.cos(ang), jnp.sin(ang)

def apply_rope(x, cos, sin):
    x1, x2 = jnp.split(x, 2, axis=-1)
    c = cos[None, :, None, :]
    s = sin[None, :, None, :]
    return jnp.concatenate([x1 * c - x2 * s, x2 * c + x1 * s], axis=-1)

def swa_attention(q, k, v, q_gain, k_gain, sinks, cos, sin):
    B, T = q.shape[0], q.shape[1]
    G = SWA_HEADS // SWA_KV_HEADS
    nb = T // SWA_BLOCK
    q = apply_rope(rmsnorm_2(q, q_gain).astype(jnp.float32), cos, sin)
    k = apply_rope(rmsnorm_2(k, k_gain).astype(jnp.float32), cos, sin)
    v = v.astype(jnp.float32)
    q = q.reshape(B, nb, SWA_BLOCK, SWA_KV_HEADS, G, SWA_HEAD_DIM)
    k = k.reshape(B, nb, SWA_BLOCK, SWA_KV_HEADS, SWA_HEAD_DIM)
    v = v.reshape(B, nb, SWA_BLOCK, SWA_KV_HEADS, SWA_HEAD_DIM)

    def band(t):
        prev = jnp.pad(t[:, :-1], ((0, 0), (1, 0), (0, 0), (0, 0), (0, 0)))
        return jnp.concatenate([prev, t], axis=2)

    kb, vb = band(k), band(v)
    s = jnp.einsum('bnqhgd,bnkhd->bnhgqk', q, kb) * (SWA_HEAD_DIM ** -0.5)
    i = jnp.arange(SWA_BLOCK)[:, None]
    j = jnp.arange(2 * SWA_BLOCK)[None, :]
    rel = i + SWA_BLOCK - j
    blk = jnp.arange(nb)[:, None, None]
    valid = (rel >= 0) & (rel < SWA_WINDOW) & ((blk > 0) | (j >= SWA_BLOCK))
    s = jnp.where(valid[None, :, None, None], s, -jnp.inf)
    sink = sinks.astype(jnp.float32).reshape(1, 1, SWA_KV_HEADS, G, 1, 1)
    m = jnp.maximum(jnp.max(s, axis=-1, keepdims=True), sink)
    p = jnp.exp(s - m)
    denom = jnp.sum(p, axis=-1, keepdims=True) + jnp.exp(sink - m)
    o = jnp.einsum('bnhgqk,bnkhd->bnqhgd', p / denom, vb)
    return o.reshape(B, T, SWA_Q_W)

def gla_attention(q, k, v, log_a):
    B, T = q.shape[0], q.shape[1]
    nc = T // GLA_CHUNK

    def chunks(t, d):
        return t.astype(jnp.float32).reshape(B, nc, GLA_CHUNK, GLA_HEADS, d).transpose(1, 0, 3, 2, 4)

    qc = chunks(q, GLA_DK) * (GLA_DK ** -0.5)
    kc = chunks(k, GLA_DK)
    vc = chunks(v, GLA_DV)
    gc = chunks(log_a, GLA_DK)
    causal = jnp.tril(jnp.ones((GLA_CHUNK, GLA_CHUNK), dtype=bool))[:, :, None]

    def step(S, inp):
        qi, ki, vi, gi = inp
        b = jnp.cumsum(gi, axis=-2)
        b_last = b[:, :, -1:, :]
        o_inter = jnp.einsum('bhtc,bhcv->bhtv', qi * jnp.exp(b), S)
        diff = b[:, :, :, None, :] - b[:, :, None, :, :]
        decay = jnp.exp(jnp.where(causal, diff, -jnp.inf))
        attn = jnp.einsum('bhtsc,bhsc->bhts', qi[:, :, :, None, :] * decay, ki)
        o_intra = jnp.einsum('bhts,bhsv->bhtv', attn, vi)
        S = jnp.exp(b_last[:, :, 0, :])[..., None] * S + jnp.einsum('bhsc,bhsv->bhcv', ki * jnp.exp(b_last - b), vi)
        return S, o_inter + o_intra

    S0 = jnp.zeros((B, GLA_HEADS, GLA_DK, GLA_DV), jnp.float32)
    _, o = lax.scan(step, S0, (qc, kc, vc, gc))
    return o.transpose(1, 0, 3, 2, 4).reshape(B, T, GLA_HEADS, GLA_DV)

def second_inputs(seed: int = 0) -> dict:
    key = jax.random.key(seed)
    ks = jax.random.split(key, 24)
    L, D = DEPTH, D_MODEL

    def w(k, shape, fan_in):
        return jax.random.normal(k, shape, jnp.float32) * (fan_in ** -0.5)

    def gain(k, shape):
        return 1.0 + 0.02 * jax.random.normal(k, shape, jnp.float32)

    return {
        "x": jax.random.normal(ks[0], (BATCH, SEQ, D), jnp.float32),
        "ffn1_norm": gain(ks[1], (L, D)),
        "ffn1_w_gate": w(ks[2], (L, D, D_FF), D),
        "ffn1_w_up": w(ks[3], (L, D, D_FF), D),
        "ffn1_w_down": w(ks[4], (L, D_FF, D), D_FF),
        "mix_norm": gain(ks[5], (L, D)),
        "w_in": w(ks[6], (L, D, IN_COLS), D),
        "swa_q_norm": gain(ks[7], (L, SWA_HEAD_DIM)),
        "swa_k_norm": gain(ks[8], (L, SWA_HEAD_DIM)),
        "swa_sinks": 0.5 * jax.random.normal(ks[9], (L, SWA_HEADS), jnp.float32),
        "gla_w_gate": w(ks[10], (L, GLA_GATE_RANK, GLA_K_W), GLA_GATE_RANK),
        "gla_gate_bias": 0.1 * jax.random.normal(ks[11], (L, GLA_K_W), jnp.float32),
        "gla_out_norm": gain(ks[12], (L, GLA_V_W)),
        "w_proj_a": w(ks[13], (L, SWA_Q_W, D), SWA_Q_W),
        "w_proj_b": w(ks[14], (L, GLA_V_W, D), GLA_V_W),
        "w_out": w(ks[15], (L, D, D), D),
        "ffn2_norm": gain(ks[16], (L, D)),
        "ffn2_w_gate": w(ks[17], (L, D, D_FF), D),
        "ffn2_w_up": w(ks[18], (L, D, D_FF), D),
        "ffn2_w_down": w(ks[19], (L, D_FF, D), D_FF),
    }

def second_block(x, ffn1_norm, ffn1_w_gate, ffn1_w_up, ffn1_w_down, mix_norm, w_in,
              swa_q_norm, swa_k_norm, swa_sinks, gla_w_gate, gla_gate_bias, gla_out_norm,
              w_proj_a, w_proj_b, w_out, ffn2_norm, ffn2_w_gate, ffn2_w_up, ffn2_w_down):
    B, T = x.shape[0], x.shape[1]
    cos, sin = rope_tables(T)
    for l in range(DEPTH):
        h = rmsnorm_2(x, ffn1_norm[l])
        x = x + 0.5 * swiglu_2(h, ffn1_w_gate[l], ffn1_w_up[l], ffn1_w_down[l])

        h = rmsnorm_2(x, mix_norm[l])
        z = h @ w_in[l]
        q_a, k_a, v_a, q_b, k_b, v_b, r_b, g_lr, gate_a, gate_b = split_cols(z, IN_SPLITS)

        o_a = swa_attention(q_a.reshape(B, T, SWA_HEADS, SWA_HEAD_DIM),
                            k_a.reshape(B, T, SWA_KV_HEADS, SWA_HEAD_DIM),
                            v_a.reshape(B, T, SWA_KV_HEADS, SWA_HEAD_DIM),
                            swa_q_norm[l], swa_k_norm[l], swa_sinks[l], cos, sin).astype(x.dtype)

        log_a = jax.nn.log_sigmoid((g_lr @ gla_w_gate[l] + gla_gate_bias[l]).astype(jnp.float32)) / GLA_TAU
        o_b = gla_attention(q_b.reshape(B, T, GLA_HEADS, GLA_DK),
                            k_b.reshape(B, T, GLA_HEADS, GLA_DK),
                            v_b.reshape(B, T, GLA_HEADS, GLA_DV),
                            log_a.reshape(B, T, GLA_HEADS, GLA_DK))
        o_b = rmsnorm_2(o_b, gla_out_norm[l].reshape(GLA_HEADS, GLA_DV)).reshape(B, T, GLA_V_W).astype(x.dtype)
        o_b = o_b * jax.nn.silu(r_b)

        y_a = o_a @ w_proj_a[l]
        y_b = o_b @ w_proj_b[l]
        merged = jax.nn.sigmoid(gate_a) * y_a + jax.nn.sigmoid(gate_b) * y_b
        x = x + merged @ w_out[l]

        h = rmsnorm_2(x, ffn2_norm[l])
        x = x + 0.5 * swiglu_2(h, ffn2_w_gate[l], ffn2_w_up[l], ffn2_w_down[l])
    return x


def setup_inputs(seed=0):
    out = dict(first_inputs(seed))
    for name, value in second_inputs(seed + 1).items():
        if name != "x":
            out[name + "_2"] = value
    return out


def reference(
    x, g_ffn1, w1_a, w3_a, w2_a, g_mix, w_in, w_fourier, w_conv, w_conv_out, w_pool, pool_scale,
    w_o, g_ffn2, w1_b, w3_b, w2_b, g_final, ffn1_norm_2, ffn1_w_gate_2, ffn1_w_up_2,
    ffn1_w_down_2, mix_norm_2, w_in_2, swa_q_norm_2, swa_k_norm_2, swa_sinks_2, gla_w_gate_2,
    gla_gate_bias_2, gla_out_norm_2, w_proj_a_2, w_proj_b_2, w_out_2, ffn2_norm_2,
    ffn2_w_gate_2, ffn2_w_up_2, ffn2_w_down_2,
):
    x = first_block(
        x, g_ffn1, w1_a, w3_a, w2_a, g_mix, w_in, w_fourier, w_conv, w_conv_out, w_pool,
        pool_scale, w_o, g_ffn2, w1_b, w3_b, w2_b, g_final,
    )
    return second_block(
        x, ffn1_norm_2, ffn1_w_gate_2, ffn1_w_up_2, ffn1_w_down_2, mix_norm_2, w_in_2,
        swa_q_norm_2, swa_k_norm_2, swa_sinks_2, gla_w_gate_2, gla_gate_bias_2, gla_out_norm_2,
        w_proj_a_2, w_proj_b_2, w_out_2, ffn2_norm_2, ffn2_w_gate_2, ffn2_w_up_2, ffn2_w_down_2,
    )


_drawn_inputs = setup_inputs


def setup_inputs(seed=0):
    import zlib

    import numpy as np

    out = dict(_drawn_inputs(seed))
    spreads = {}
    factors = {'g_ffn1': 2.735,
     'pool_scale': 3.76,
     'g_ffn2': 4.143,
     'ffn1_norm_2': 3.945,
     'mix_norm_2': 2.931,
     'swa_q_norm_2': 8.0,
     'swa_k_norm_2': 8.0,
     'swa_sinks_2': 171.984,
     'gla_gate_bias_2': 2.802,
     'gla_out_norm_2': 6.006,
     'ffn2_norm_2': 4.879}
    for name, (base, spread) in spreads.items():
        noise = np.random.default_rng([zlib.crc32(name.encode()), seed]).standard_normal(out[name].shape)
        drawn = base * np.exp(spread * noise) if base else spread * noise
        out[name] = __import__('jax').numpy.asarray(drawn.astype(out[name].dtype))
    for name, factor in factors.items():
        out[name] = (out[name] * factor).astype(out[name].dtype)
    return out
```

```python
import concourse.bass as bass
from concourse import mybir
from contextlib import ExitStack, contextmanager
import numpy as np

F32 = mybir.dt.float32
F32R = mybir.dt.float32r
I32 = mybir.dt.int32
ACT = mybir.ActivationFunctionType
ALU = mybir.AluOpType
AX_X = mybir.AxisListType.X

P = 128
T = 256
MT = T // P
D = 1024
DC = D // P
FF = 2816
FG = FF // 256
FC = FF // P
EPS = 1e-6
RAW = 2
HL = 4

LAYERS = 2
FFN_UNITS = 2 * FG + 12
MIX_UNITS = {1: 32, 2: 36}
LAYER_UNITS = {b: 2 * FFN_UNITS + MIX_UNITS[b] for b in (1, 2)}
SHORT = {1: {FFN_UNITS + u: 512 for u in (12, 15, 21, 24)},
         2: {FFN_UNITS + 3: 128} | {FFN_UNITS + u: 1024 for u in range(20, 24)}}
for b in (1, 2):
    for u in (0, FFN_UNITS + MIX_UNITS[b]):
        SHORT[b].update({u + FFN_UNITS - 7: 1024, u + FFN_UNITS - 1: 1024})
UNITS_BEFORE = {"start": 0, 1: 0, "between": LAYERS * LAYER_UNITS[1], 2: LAYERS * LAYER_UNITS[1]}
assert all(n % HL == 0 and n % RAW == 0 for n in LAYER_UNITS.values())
SEGMENTS = (("start", 1), (1, LAYERS), ("between", 1), (2, LAYERS), ("end", 1))
OFF_F, OFF_B, OFF_C, OFF_V, OFF_P, OFF_G = range(0, 6 * 512, 512)
VEC_ROWS = {1: (("g_ffn1", DC), ("g_mix", DC), ("g_ffn2", DC), ("w_conv", 12)),
            2: (("ffn1_norm_2", DC), ("mix_norm_2", DC), ("ffn2_norm_2", DC), ("gla_out_norm_2", DC))}
VR = {b: LAYERS * sum(n for _, n in VEC_ROWS[b]) for b in (1, 2)}
VL = max(VR.values()) // LAYERS
V_GAIN = {"ffn0": 0, "mix": DC, "ffn1": 2 * DC}
V_CONV = V_OUT_NORM = 3 * DC
N_CONSTS = 3 + 8
HEADS, KV_HEADS, HEAD_DIM = 8, 2, 64
QK_HEADS = HEADS + 2 * KV_HEADS
QK = QK_HEADS * HEAD_DIM
GLA_HEADS, DK, DV, RANK = 4, 128, 256, 16
TAU = 16.0
IN2 = {"qa": 0, "kv": 512, "qb": 768, "kb": 1280, "vb": 1792, "rb": 2816, "glr": 3840, "ga": 3856, "gb": 4880}
LEVELS = 8
N_MIX2 = 9


class Counts:

    def __init__(self):
        self.labels, self.totals, self.names = {}, {}, {}

    def __eq__(self, other):
        return (self.labels, self.totals) == (other.labels, other.totals)


class Engine:

    def __init__(self, eng, counts, known, own=None):
        self.eng, self.counts, self.known, self.own = eng, counts, known, own
        self.segment, self.lay, self.it, self.raised = "start", None, None, {}

    def in_layer(self, first, per_layer, per_turn=0):
        out = first
        if self.lay is not None and per_layer:
            out = self.lay * per_layer + out
        if self.it is not None and per_turn:
            out = self.it * per_turn + out
        return out

    def mark(self, semaphore, label):
        name = self.counts.names[id(semaphore)]
        self.raised[name] = self.raised.get(name, 0) + 1
        key = (name, self.segment, label)
        assert key not in self.counts.labels, key
        self.counts.labels[key] = self.raised[name]
        return 1

    def after(self, semaphore, label):
        if self.known is None:
            return 1
        name = self.counts.names[id(semaphore)]
        totals = self.known.totals
        before = 0
        for segment, times in SEGMENTS:
            if segment == self.segment:
                break
            before += times * totals.get((name, segment), 0)
        return self.in_layer(before + self.known.labels[(name, self.segment, label)],
                             totals.get((name, self.segment), 0))

    def link(self, ins):
        label = ("own", self.raised.get(self.counts.names[id(self.own)], 0))
        ins.then_inc(self.own, self.mark(self.own, label))
        self.eng.wait_ge(self.own, self.after(self.own, label))

    def enter(self, segment):
        for name, n in self.raised.items():
            self.counts.totals[(name, self.segment)] = n
        self.segment, self.lay, self.raised = segment, None, {}

    @contextmanager
    def layers(self, segment):
        self.enter(segment)
        with self.eng.Fori(0, LAYERS) as self.lay:
            yield
        self.lay = None

    @contextmanager
    def turns(self, n):
        with self.eng.Fori(0, n) as self.it:
            yield
        self.it = None


SMALL_OPS = (
    [("glt",), ("loga", 0), ("loga", 1), ("kb", 0), ("kb", 1), ("qb", 0), ("qb", 1)] + [("qkt", j) for j in range(3)]
    + [("score", h) for h in range(HEADS)] + [("ex", 0, part, m) for part in range(2) for m in range(MT)]
    + [("prob_t", j) for j in range(4)]
    + [("weights", 0, 0), ("weights", 0, 1), ("prob_t", 4), ("weights", 0, 2), ("weights", 0, 3), ("cross", 0),
       ("prob_t", 5)]
    + [("ex", 1, 0, 0), ("ex", 1, 0, 1), ("oa", 0), ("oa", 1), ("ex", 1, 1, 0), ("ex", 1, 1, 1)]
    + [("oat", 0), ("oat", 1), ("ob", 0)] + [("weights", 1, i) for i in range(4)] + [("cross", 1)]
    + [("ex", 2, part, m) for part in range(2) for m in range(MT)] + [("ob", 1)]
    + [("weights", 2, i) for i in range(4)] + [("cross", 2)]
    + [("ex", 3, part, m) for part in range(2) for m in range(MT)] + [("ob", 2)]
    + [("weights", 3, i) for i in range(4)] + [("cross", 3), ("ob", 3)]
    + [("obt", j) for j in range(4)] + [("mt", n, j) for n in range(2) for j in range(2)])
FOUR_BANKS = SMALL_OPS.index(("weights", 1, 2))
BANK = {op: (6, 7, 4, 5)[i % 4] if i < FOUR_BANKS else (6, 7)[i % 2] for i, op in enumerate(SMALL_OPS)}
READ_BY_SCALAR = ("glt", "kb", "qb", "qkt", "prob_t", "ex", "cross")


def previous_in_bank(op):
    before = [o for o in SMALL_OPS[:SMALL_OPS.index(op)] if BANK[o] == BANK[op]]
    return before[-1] if before else None


def build(nc, a, known):
    ctx = ExitStack()
    counts = Counts()

    def semaphore(name):
        return ctx.enter_context(nc.semaphore(name))

    def signal(name):
        out = semaphore(name)
        counts.names[id(out)] = name
        return out

    with ctx:
        def sb(stack, name, shape, dt=F32):
            return stack.enter_context(nc.sbuf_tensor(name, shape, dt))

        raw = sb(ctx, "raw", [P, RAW, 2048])
        whi = sb(ctx, "whi", [P, HL, 2048], F32R)
        wlo = sb(ctx, "wlo", [P, HL, 2048], F32R)
        x = sb(ctx, "x", [P, MT, D])
        xt_hi = sb(ctx, "xt_hi", [P, DC, T], F32R)
        xt_lo = sb(ctx, "xt_lo", [P, DC, T], F32R)
        ident = sb(ctx, "ident", [P, P])
        vecs = sb(ctx, "vecs", [P, VR[1] + VR[2] + VR[2] // LAYERS])
        v = sb(ctx, "v", [P, VL])
        ss = sb(ctx, "ss", [P, MT])
        ms = sb(ctx, "ms", [P, MT])
        rt = sb(ctx, "rt", [P, MT])
        rstd = sb(ctx, "rstd", [P, MT])
        nt = sb(ctx, "nt", [P, 2, MT])
        psum = ctx.enter_context(nc.psum_tensor("psum", [P, 8, 512], F32))

        ffn = ExitStack()
        ht_hi = sb(ffn, "ht_hi", [P, FC, T], F32R)
        ht_lo = sb(ffn, "ht_lo", [P, FC, T], F32R)
        gate = sb(ffn, "gate", [P, MT, 256])
        hid = sb(ffn, "hid", [P, MT, 256])
        junk = sb(ffn, "junk", [P, MT, D])
        vrows = sb(ffn, "vrows", [P, 2, P])
        gfin = sb(ffn, "gfin", [P, D])
        ffn.close()

        mix1 = ExitStack()
        bz_hi, bz_lo = (sb(mix1, n, [P, 4, T], F32R) for n in ("bz_hi", "bz_lo"))
        fq_hi, fq_lo = (sb(mix1, n, [P, 4, T], F32R) for n in ("fq_hi", "fq_lo"))
        pl_hi, pl_lo = (sb(mix1, n, [P, 4, T], F32R) for n in ("pl_hi", "pl_lo"))
        mt1_hi, mt1_lo = (sb(mix1, n, [P, DC, T], F32R) for n in ("mt1_hi", "mt1_lo"))
        cs = sb(mix1, "cs", [P, MT, 512])
        cc = sb(mix1, "cc", [P, 256])
        poolm = sb(mix1, "poolm", [P, MT, 4, T])
        pscale = sb(mix1, "pscale", [P, D])
        sig1 = sb(mix1, "sig1", [P, MT, 512])
        merged1 = sb(mix1, "merged1", [P, MT, 512])
        part1 = sb(mix1, "part1", [P, 512])
        tok = sb(mix1, "tok", [P, MT, 512])
        ptok = sb(mix1, "ptok", [P, MT, 512])
        ab = sb(mix1, "ab", [P, 4, 512])
        z = sb(mix1, "z", [P, MT, 512])
        zt = sb(mix1, "zt", [P, 4, T + 2])
        cv = sb(mix1, "cv", [P, 4, T])
        mix1.close()

        mix2 = ExitStack()

        def overlay(*sets):
            out = {}
            for tensors in sets[1:] + sets[:1]:
                stack = mix2 if tensors is sets[0] else ExitStack()
                for name, shape, dt in tensors:
                    out[name] = sb(stack, name, shape, dt)
                if stack is not mix2:
                    stack.close()
            return out
        oa_hi, oa_lo = (sb(mix2, n, [P, 4, T], F32R) for n in ("oa_hi", "oa_lo"))
        t2 = overlay(
            [("ob_hi", [P, DC, T], F32R), ("ob_lo", [P, DC, T], F32R)],
            [("xg", [P, 2, LEVELS, T], F32)],
            [("softplus", [P, MT, 512], F32), ("gl", [P, MT, RANK], F32), ("glt", [P, T], F32)])
        t2.update(overlay(
            [("mt2_hi", [P, DC, T], F32R), ("mt2_lo", [P, DC, T], F32R)],
            [("vb", [P, MT, D], F32), ("rb", [P, MT, D], F32)],
            [("qk", [P, MT, QK], F32), ("qkr", [P, MT, QK], F32), ("rope_t", [P, 2, QK // 2], F32)]))
        t2.update(overlay(
            [("merged2", [P, MT, D], F32), ("sig2", [P, MT, D], F32)],
            [("prob", [P, HEADS, 3, P], F32)]))
        t2.update(overlay(
            [("prob_t", [P, 3 * HEADS, P], F32)],
            [("qkt", [P, QK // P, T], F32)]))
        t2.update(overlay(
            [("tok2", [P, MT, 512], F32)],
            [("oa", [P, MT, 512], F32)],
            [("part2", [P, MT, 512], F32)]))
        ob_hi, ob_lo, xg, softplus, gl, glt = (t2[n] for n in ("ob_hi", "ob_lo", "xg", "softplus", "gl", "glt"))
        mt2_hi, mt2_lo, vb, rb, qk, qkr, rope_t = (
            t2[n] for n in ("mt2_hi", "mt2_lo", "vb", "rb", "qk", "qkr", "rope_t"))
        merged2, sig2, prob, prob_t, qkt = (t2[n] for n in ("merged2", "sig2", "prob", "prob_t", "qkt"))
        tok2, oa, part2 = (t2[n] for n in ("tok2", "oa", "part2"))
        va = sb(mix2, "va", [P, MT, P])
        qbt = sb(mix2, "qbt", [P, GLA_HEADS, T])
        kbt = sb(mix2, "kbt", [P, GLA_HEADS, T])
        loga = sb(mix2, "loga", [P, MT, 512])
        pg = sb(mix2, "pg", [P, MT, P])
        px = sb(mix2, "px", [P, P])
        spans = sb(mix2, "spans", [P, 3, 512])
        pairs = sb(mix2, "pairs", [P, LEVELS, P])
        window = sb(mix2, "window", [P, 3 * P])
        rope = sb(mix2, "rope", [P, MT, 2, 32])
        qk_gain = sb(mix2, "qk_gain", [P, 2, HEAD_DIM])
        sinks = sb(mix2, "sinks", [P, HEADS])
        gwb = sb(mix2, "gwb", [RANK + 1, 512])
        s24 = sb(mix2, "s24", [P, 4, MT * QK_HEADS])
        mx = sb(mix2, "mx", [P, HEADS, 2])
        nm = sb(mix2, "nm", [P, HEADS, 2])
        dm = sb(mix2, "dm", [P, HEADS, 2])
        rs = sb(mix2, "rs", [P, HEADS, 2])
        so = sb(mix2, "so", [P, 5, MT * GLA_HEADS])
        so_junk = sb(mix2, "so_junk", [P, DV], mybir.dt.bfloat16)
        mix2.close()

        raw_in = [semaphore(f"raw_in{r}") for r in range(RAW)]
        hi_done = semaphore("hi_done")
        w_ready = semaphore("w_ready")
        w_used = semaphore("w_used")
        gate_done = semaphore("gate_done")
        hid_done = semaphore("hid_done")
        ht_ready = semaphore("ht_ready")
        ht_hi_done = semaphore("ht_hi_done")
        ht_done = semaphore("ht_done")
        x_whole = semaphore("x_whole")
        x_half = semaphore("x_half")
        consts_in = semaphore("consts_in")
        mix_in = semaphore("mix_in")
        gfin_in = semaphore("gfin_in")
        stored = semaphore("stored")
        small = signal("small")
        acted = signal("acted")
        done = signal("done")
        act_own = signal("act_own")
        dve_own = signal("dve_own")

        def units(e, u, extra=0):
            return e.in_layer(UNITS_BEFORE[e.segment] + u + 1 + extra, LAYER_UNITS.get(e.segment, 0), 4)

        def loaded(e, u):
            return e.in_layer(32 * (UNITS_BEFORE[e.segment] // RAW + u // RAW + 1),
                              32 * LAYER_UNITS.get(e.segment, 0) // RAW, 32 * 4 // RAW)

        def groups(e, f, g, extra=0):
            first = {1: 0, 2: 2 * LAYERS * FG}[e.segment]
            return e.in_layer(first + f * FG + g + 1 + extra, 2 * FG, 2)

        def gates(e, f, g, m):
            first = {1: 0, 2: 4 * LAYERS * FG}[e.segment]
            return e.in_layer(first + 2 * (f * FG + g) + m + 1, 4 * FG, 4)

        def wholes(e):
            return e.in_layer({1: 1, "between": 1 + LAYERS, 2: 2 + LAYERS, "end": 2 + 2 * LAYERS}[e.segment], 1)

        def halves(e):
            return e.in_layer({1: 1, 2: 2 + LAYERS}[e.segment], 1)

        def mix_tables(e):
            return e.in_layer({1: 16 * 4, 2: 16 * 4 * LAYERS + 16 * N_MIX2}[e.segment],
                              16 * {1: 4, 2: N_MIX2}[e.segment])

        block = ctx.enter_context(nc.Block())

        @block.sync
        def _(eng):
            e = Engine(eng, counts, known)

            def load(u, halves):
                r = u % RAW
                eng.wait_ge(w_ready, units(e, u))
                for dst, src in halves:
                    eng.dma_start(dst(raw[:, r, :]), src).then_inc(raw_in[r], 16)

            def gate_up(w1, w3, row, col, u):
                def part(j):
                    return lambda slot: slot.rearrange("p (k n) -> p k n", k=4)[:, :, 256 * j:256 * j + 256]
                load(u, [(part(j), w[bass.ds(row, 4 * P), col].rearrange("(k p) n -> p k n", p=P))
                         for j, w in enumerate((w1, w3))])

            def plain(w, per_layer, row, col, u, chunks=4, cols=512):
                k = chunks // 2
                rows = [eng.snap(e.lay * per_layer + (row + j * k * P)) for j in range(2)]

                def part(j):
                    return lambda slot: slot[:, j * k * cols:(j + 1) * k * cols].rearrange("p (k n) -> p k n", k=k)
                load(u, [(part(j), w[bass.ds(rows[j], k * P), col:col + cols].rearrange("(k p) n -> p k n", p=P))
                         for j in range(2)])

            def wide(w, u, col, cols=512):
                for k in range(2):
                    plain(w, D, 4 * P * k, col, u + k, 4, cols)

            def flat(w):
                return w.rearrange("l k n -> (l k) n")

            def ffn_loads(u0, w1, w3, w2):
                w1, w3, w2 = flat(w1), flat(w3), flat(w2)
                rows = [eng.snap(e.lay * D + 4 * P * k) for k in range(2)]
                for k in range(2):
                    gate_up(w1, w3, rows[k], slice(0, 256), u0 + k)
                with e.turns((FG - 1) // 2):
                    rows = [eng.snap(e.lay * D + 4 * P * k) for k in range(2)]
                    cols = [eng.snap(e.it * 512 + 256 * j) for j in (1, 2)]
                    for j in range(2):
                        for k in range(2):
                            gate_up(w1, w3, rows[k], bass.ds(cols[j], 256), u0 + 2 + 2 * j + k)
                for half in range(2):
                    for i in range(6):
                        plain(w2, FF, 4 * P * i, 512 * half, u0 + 2 * FG + 6 * half + i, 4 if i < 5 else 2)

            def mix1_loads(u0):
                w_in = flat(a["w_in"])
                for i, col in enumerate((OFF_F, OFF_P, OFF_C, OFF_V, OFF_B)):
                    wide(w_in, u0 + 2 * i, col)
                for n in range(2):
                    u = u0 + 10 + 9 * n
                    wide(w_in, u, OFF_G + 512 * n)
                    plain(a["w_fourier"].rearrange("l g c d -> (l g c) d"), 512, 256 * n, 0, u + 2, 2, 256)
                    wide(w_in, u + 3, OFF_G + 2 * D + 512 * n)
                    plain(a["w_pool"].rearrange("l g c d -> (l g c) d"), 512, 256 * n, 0, u + 5, 2, 256)
                    wide(w_in, u + 6, OFF_G + D + 512 * n)
                    plain(flat(a["w_conv_out"]), 512, 0, 512 * n, u + 8)
                for n in range(2):
                    wide(flat(a["w_o"]), u0 + 28 + 2 * n, 512 * n)

            def mix2_loads(u0):
                w_in = flat(a["w_in_2"])
                wide(w_in, u0, IN2["qa"])
                plain(w_in, D, 0, IN2["kv"], u0 + 2, 8, 256)
                plain(w_in, D, 0, IN2["glr"], u0 + 3, 8, RANK)
                for i, col in enumerate((IN2["kb"], IN2["qb"], IN2["vb"], IN2["vb"] + 512, IN2["rb"], IN2["rb"] + 512,
                                         IN2["ga"], IN2["ga"] + 512)):
                    wide(w_in, u0 + 4 + 2 * i, col)
                for n in range(2):
                    for k in range(2):
                        plain(flat(a["w_proj_a_2"]), 512, 2 * P * k, 512 * n, u0 + 20 + 2 * n + k, 2)
                for n in range(2):
                    wide(w_in, u0 + 24 + 2 * n, IN2["gb"] + 512 * n)
                for n in range(2):
                    wide(flat(a["w_proj_b_2"]), u0 + 28 + 2 * n, 512 * n)
                for n in range(2):
                    wide(flat(a["w_out_2"]), u0 + 32 + 2 * n, 512 * n)

            for m in range(MT):
                eng.dma_start(x[:, m, :], a["x"][0, m * P:(m + 1) * P, :]).then_inc(consts_in, 16)
            eng.dma_start(ident[:, :], a["t_ident"]).then_inc(consts_in, 16)
            for b in (1, 2):
                at = 0
                for name, rows in VEC_ROWS[b]:
                    src = a[name].rearrange("l (c p) -> (l c) p", p=P) if len(a[name].shape) == 2 else \
                        a[name].rearrange("l k (c p) -> (l k c) p", p=P)
                    eng.dma_start(vrows[at:at + LAYERS * rows, b - 1, :], src).then_inc(consts_in, 16)
                    at += LAYERS * rows
            with e.layers(1):
                ffn_loads(0, a["w1_a"], a["w3_a"], a["w2_a"])
                mix1_loads(FFN_UNITS)
                ffn_loads(FFN_UNITS + MIX_UNITS[1], a["w1_b"], a["w3_b"], a["w2_b"])
            e.enter("between")
            with e.layers(2):
                ffn_loads(0, a["ffn1_w_gate_2"], a["ffn1_w_up_2"], a["ffn1_w_down_2"])
                mix2_loads(FFN_UNITS)
                ffn_loads(FFN_UNITS + MIX_UNITS[2], a["ffn2_w_gate_2"], a["ffn2_w_up_2"], a["ffn2_w_down_2"])
            for u in range(3):
                eng.wait_ge(w_ready, LAYERS * sum(LAYER_UNITS[b] for b in (1, 2)) + u + 1)
                eng.sem_inc(raw_in[u % RAW], 32)
            e.enter("end")
            eng.wait_ge(x_whole, wholes(e))
            for m in range(MT):
                eng.dma_start(a["out"][0, m * P:(m + 1) * P, :], x[:, m, :]).then_inc(stored, 16)
            eng.wait_ge(stored, 32)

        @block.tensor
        def _(eng):
            e = Engine(eng, counts, known)

            XT, HT = (xt_hi, xt_lo), (ht_hi, ht_lo)

            def pair(p, m):
                return psum[:, 2 * p + m, :]

            def blocks(u, block, p, split, chunks, start, stop, used, cols=512, beside=False):
                hi, lo = split
                slot = u % HL
                if block == 0:
                    eng.wait_ge(w_ready, units(e, u, RAW))
                for i, c in enumerate(chunks):
                    w = slice((block + i) * cols, (block + i + 1) * cols)
                    out = w if beside else slice(0, cols)
                    first = start and (beside or i == 0)
                    final = stop and (beside or i == len(chunks) - 1)
                    for m in range(MT):
                        t = slice(m * P, (m + 1) * P)
                        nc.tensor.matmul(pair(p, m)[:, out], hi[:, c, t], whi[:, slot, w], start=first, stop=False)
                        nc.tensor.matmul(pair(p, m)[:, out], hi[:, c, t], wlo[:, slot, w], start=False, stop=False)
                        last = nc.tensor.matmul(pair(p, m)[:, out], lo[:, c, t], whi[:, slot, w],
                                                start=False, stop=final)
                if used:
                    last.then_inc(w_used, 1)

            def wide(u, p, split, first=0, end=4):
                for q in range(first, end):
                    blocks(u + q // 2, q % 2 * 2, p, split, (2 * q, 2 * q + 1), q == 0, q == 3, q % 2 == 1)

            def turn(bank, tiles):
                for i, tile in enumerate(tiles):
                    for m in range(MT):
                        src = tile(m)
                        last = nc.tensor.transpose(bank[0:src.shape[1], i * T + m * P:i * T + (m + 1) * P],
                                                   src, ident[:, :])
                return last

            def chunk(src, c):
                return lambda m: src[:, m, c * P:(c + 1) * P]

            def x_transposes(stage, half):
                for j in range(2):
                    c = 4 * half + 2 * j
                    turn(psum[:, 6 + j, :], (chunk(x, c), chunk(x, c + 1))).then_inc(
                        small, e.mark(small, ("xt", stage, half, j)))

            def stage_first(u0, stage):
                if stage == "ffn0":
                    eng.wait_ge(x_half, halves(e))
                else:
                    eng.wait_ge(done, e.after(done, ("xt", stage, 0, 1)))
                wide(u0, 0, XT, 0, 1)
                if stage == "ffn0":
                    eng.wait_ge(x_whole, wholes(e))
                else:
                    eng.wait_ge(done, e.after(done, ("x", stage, 1)))
                x_transposes(stage, 1)
                wide(u0, 0, XT, 1, 2)
                eng.wait_ge(done, e.after(done, ("xt", stage, 1, 1)))
                wide(u0, 0, XT, 2, 4)

            def ffn_tensor(u0, f, next_stage):
                stage = f"ffn{f}"

                def hidden_transposes(g):
                    eng.wait_ge(hid_done, groups(e, f, g, 2))
                    eng.wait_ge(ht_done, groups(e, f, g - 2, 2))
                    turn(psum[:, 6 + g % 2, :], (chunk(hid, 0), chunk(hid, 1))).then_inc(ht_ready, 1)

                stage_first(u0, stage)
                with e.turns((FG - 1) // 2):
                    for g in (1, 2):
                        eng.wait_ge(hid_done, groups(e, f, g - 2, 2))
                        wide(u0 + 2 * g, g % 2, XT, 0, 1)
                        hidden_transposes(g - 1)
                        wide(u0 + 2 * g, g % 2, XT, 1, 4)
                u = u0 + 2 * FG
                eng.wait_ge(ht_done, groups(e, f, FG - 2, 2))
                blocks(u, 0, 2, HT, (0, 1), True, False, False)
                hidden_transposes(FG - 1)
                blocks(u, 2, 2, HT, (2, 3), False, False, True)
                for i in range(1, 5):
                    blocks(u + i, 0, 2, HT, range(4 * i, 4 * i + 4), False, False, True)
                eng.wait_ge(ht_done, groups(e, f, FG - 1, 2))
                blocks(u + 5, 0, 2, HT, (20, 21), False, True, True)
                u += 6
                blocks(u, 0, 1, HT, (0, 1), True, False, False)
                eng.wait_ge(done, e.after(done, ("x", next_stage, 0)))
                x_transposes(next_stage, 0)
                blocks(u, 2, 1, HT, (2, 3), False, False, True)
                for i in range(1, 5):
                    blocks(u + i, 0, 1, HT, range(4 * i, 4 * i + 4), False, False, True)
                blocks(u + 5, 0, 1, HT, (20, 21), False, True, True)

            def mix1_tensor(u0):
                MERGED = (mt1_hi, mt1_lo)

                def dft_tokens(g):
                    for m in range(MT):
                        last = nc.tensor.matmul(psum[:, 6 + g % 2, :], tok[:, m, g * P:(g + 1) * P], cs[:, m, :],
                                                start=m == 0, stop=m == 1)
                    last.then_inc(small, e.mark(small, ("ab", g)))

                def dft_channels(j):
                    for i in range(2):
                        out = psum[:, 6 + j, i * T:(i + 1) * T]
                        nc.tensor.matmul(out, cc[:, 0:P], ab[:, 2 * j + i, 0:T], start=True, stop=False)
                        last = nc.tensor.matmul(out, cc[:, P:2 * P], ab[:, 2 * j + i, T:2 * T], start=False, stop=True)
                    last.then_inc(small, e.mark(small, ("fq", j)))

                def pool_groups(j):
                    for i in range(2):
                        g = 2 * j + i
                        for m in range(MT):
                            last = nc.tensor.matmul(psum[:, 6 + j, i * T:(i + 1) * T], ptok[:, m, g * P:(g + 1) * P],
                                                    poolm[:, m, g, :], start=m == 0, stop=m == 1)
                    last.then_inc(small, e.mark(small, ("pl", j)))

                def turns(label, src):
                    for j in range(2):
                        turn(psum[:, 6 + j, :], (chunk(src, 2 * j), chunk(src, 2 * j + 1))).then_inc(
                            small, e.mark(small, (label, j)))

                u = u0
                stage_first(u, "mix")
                u += 2
                wide(u, 1, XT, 0, 1)
                eng.wait_ge(acted, e.after(acted, ("tok", "F")))
                eng.wait_ge(mix_in, mix_tables(e))
                dft_tokens(0)
                dft_tokens(1)
                wide(u, 1, XT, 1, 3)
                for g in (2, 3):
                    eng.wait_ge(acted, e.after(acted, ("ab", g - 2)))
                    dft_tokens(g)
                wide(u, 1, XT, 3, 4)
                u += 2
                wide(u, 0, XT, 0, 1)
                for j in range(2):
                    eng.wait_ge(acted, e.after(acted, ("ab", 2 + j)))
                    dft_channels(j)
                wide(u, 0, XT, 1, 3)
                eng.wait_ge(acted, e.after(acted, ("tok", "P")))
                for j in range(2):
                    eng.wait_ge(done, e.after(done, ("fq", j)))
                    pool_groups(j)
                wide(u, 0, XT, 3, 4)
                u += 2
                wide(u, 1, XT)
                u += 2
                eng.wait_ge(acted, e.after(acted, ("tok", "C")))
                wide(u, 0, XT, 0, 1)
                eng.wait_ge(done, e.after(done, ("pl", 1)))
                eng.wait_ge(done, e.after(done, ("z", 1)))
                turns("zt", z)
                wide(u, 0, XT, 1, 4)
                u += 2
                wide(u, 1, XT, 0, 1)
                eng.wait_ge(acted, e.after(acted, ("tok", "B")))
                eng.wait_ge(acted, e.after(acted, ("zt", 1)))
                turns("bt", tok)
                wide(u, 1, XT, 1, 4)
                blocks(u + 2, 0, 2, (fq_hi, fq_lo), (0, 1), True, True, True, 256, beside=True)
                u += 3
                wide(u, 0, XT)
                eng.wait_ge(done, e.after(done, ("merged", 0, "f")))
                blocks(u + 2, 0, 2, (pl_hi, pl_lo), (0, 1), True, True, True, 256, beside=True)
                u += 3
                eng.wait_ge(acted, e.after(acted, ("sig", 0, "f")))
                wide(u, 1, XT)
                eng.wait_ge(done, e.after(done, ("merged", 0, "p")))
                eng.wait_ge(done, e.after(done, ("bz", 1)))
                blocks(u + 2, 0, 2, (bz_hi, bz_lo), range(4), True, True, True)
                u += 3
                eng.wait_ge(acted, e.after(acted, ("sig", 0, "p")))
                wide(u, 0, XT, 0, 2)
                eng.wait_ge(done, e.after(done, ("merged", 0, "c")))
                turns("mt0", merged1)
                wide(u, 0, XT, 2, 4)
                blocks(u + 2, 0, 2, (fq_hi, fq_lo), (2, 3), True, True, True, 256, beside=True)
                u += 3
                eng.wait_ge(acted, e.after(acted, ("sig", 0, "c")))
                wide(u, 1, XT)
                eng.wait_ge(done, e.after(done, ("merged", 1, "f")))
                blocks(u + 2, 0, 2, (pl_hi, pl_lo), (2, 3), True, True, True, 256, beside=True)
                u += 3
                eng.wait_ge(acted, e.after(acted, ("sig", 1, "f")))
                wide(u, 0, XT)
                eng.wait_ge(done, e.after(done, ("merged", 1, "p")))
                blocks(u + 2, 0, 2, (bz_hi, bz_lo), range(4), True, True, True)
                u += 3
                eng.wait_ge(done, e.after(done, ("mt0", 1)))
                eng.wait_ge(acted, e.after(acted, ("sig", 1, "c")))
                wide(u, 0, MERGED, 0, 1)
                eng.wait_ge(done, e.after(done, ("merged", 1, "c")))
                turns("mt1", merged1)
                wide(u, 0, MERGED, 1, 2)
                eng.wait_ge(done, e.after(done, ("mt1", 1)))
                wide(u, 0, MERGED, 2, 4)
                u += 2
                wide(u, 1, MERGED, 0, 1)
                eng.wait_ge(done, e.after(done, ("x", "ffn1", 0)))
                x_transposes("ffn1", 0)
                wide(u, 1, MERGED, 1, 4)
                assert u + 2 == u0 + MIX_UNITS[1]

            def mix2_tensor(u0):
                MERGED, OA, OB = (mt2_hi, mt2_lo), (oa_hi, oa_lo), (ob_hi, ob_lo)

                def bank(op):
                    before = previous_in_bank(op)
                    if before is not None:
                        reader = acted if before[0] in READ_BY_SCALAR else done
                        eng.wait_ge(reader, e.after(reader, before))
                    return psum[:, BANK[op], :]

                def turn_two(op, src, c):
                    turn(bank(op), (chunk(src, c), chunk(src, c + 1))).then_inc(small, e.mark(small, op))

                def score(h):
                    out = bank(("score", h))
                    d = slice(h % 2 * HEAD_DIM, (h % 2 + 1) * HEAD_DIM)
                    q, k = qkt[d, h // 2, :], qkt[d, HEADS // 2 + h // 4, :]
                    nc.tensor.matmul(out[:, 0:P], q[:, 0:P], k[:, 0:P], start=True, stop=True)
                    nc.tensor.matmul(out[:, P:3 * P], q[:, P:T], k, start=True, stop=True).then_inc(
                        small, e.mark(small, ("score", h)))

                def prob_turn(j):
                    out = bank(("prob_t", j))
                    for i in range(4):
                        h, b = divmod(4 * j + i, 3)
                        last = nc.tensor.transpose(out[:, i * P:(i + 1) * P], prob[:, h, b, :], ident[:, :])
                    last.then_inc(small, e.mark(small, ("prob_t", j)))

                def attention(b):
                    out = bank(("oa", b))
                    for h in range(HEADS):
                        d = slice(h // 4 * HEAD_DIM, (h // 4 + 1) * HEAD_DIM)
                        head = out[:, h * HEAD_DIM:(h + 1) * HEAD_DIM]
                        last = nc.tensor.matmul(head, prob_t[:, 3 * h + b, :], va[:, 0, d], start=True, stop=b == 0)
                        if b == 1:
                            last = nc.tensor.matmul(head, prob_t[:, 3 * h + 2, :], va[:, 1, d], start=False, stop=True)
                    last.then_inc(small, e.mark(small, ("oa", b)))

                def exponents(h, part):
                    for m in range(MT):
                        out = bank(("ex", h, part, m))
                        nc.tensor.matmul(out, loga[:, m, h * DK:(h + 1) * DK], spans[:, part and 1 + m, :],
                                         start=True, stop=True).then_inc(small, e.mark(small, ("ex", h, part, m)))

                def weights(h, i):
                    eng.wait_ge(done, e.after(done, ("decayed", h, i // 2)))
                    out = bank(("weights", h, i))
                    for k in range(2):
                        for m in range(MT):
                            t = slice(m * P, (m + 1) * P)
                            lv = 2 * i + k
                            keys = kbt[:, h, t] if lv == 7 else xg[:, h % 2, lv, t]
                            queries = qbt[:, h, t] if lv == 7 else xg[:, h % 2, lv, t]
                            last = nc.tensor.matmul(out[:, (2 * k + m) * P:(2 * k + m + 1) * P], keys, queries,
                                                    start=True, stop=True)
                    last.then_inc(small, e.mark(small, ("weights", h, i)))

                def cross(h):
                    nc.tensor.matmul(bank(("cross", h))[:, 0:P], xg[:, h % 2, 7, 0:P], xg[:, h % 2, 7, P:T],
                                     start=True, stop=True).then_inc(small, e.mark(small, ("cross", h)))

                def linear_out(h):
                    eng.wait_ge(done, e.after(done, ("weights", h, 3)))
                    eng.wait_ge(acted, e.after(acted, ("cross", h)))
                    out = bank(("ob", h))
                    d = slice(h * DV, (h + 1) * DV)
                    nc.tensor.matmul(out[:, 0:DV], pg[:, 0, :], vb[:, 0, d], start=True, stop=True)
                    nc.tensor.matmul(out[:, DV:2 * DV], px[:, :], vb[:, 0, d], start=True, stop=False)
                    nc.tensor.matmul(out[:, DV:2 * DV], pg[:, 1, :], vb[:, 1, d], start=False, stop=True).then_inc(
                        small, e.mark(small, ("ob", h)))

                stage_first(u0, "mix")
                blocks(u0 + 2, 0, 1, XT, range(8), True, True, True, 256)
                blocks(u0 + 3, 0, 2, XT, range(8), True, True, True, RANK)
                eng.wait_ge(acted, e.after(acted, ("qa",)))
                u = u0 + 4
                wide(u, 0, XT, 0, 3)
                eng.wait_ge(acted, e.after(acted, ("gl",)))
                turn(bank(("glt",)), (lambda m: gl[:, m, :],)).then_inc(small, e.mark(small, ("glt",)))
                wide(u, 0, XT, 3, 4)
                eng.wait_ge(acted, e.after(acted, ("kv",)))
                u += 2
                wide(u, 1, XT, 0, 1)
                eng.wait_ge(acted, e.after(acted, ("glt",)))
                eng.wait_ge(mix_in, mix_tables(e))
                for m in range(MT):
                    nc.tensor.matmul(bank(("loga", m)), glt[0:RANK + 1, m * P:(m + 1) * P], gwb[:, :],
                                     start=True, stop=True).then_inc(small, e.mark(small, ("loga", m)))
                wide(u, 1, XT, 1, 3)
                eng.wait_ge(acted, e.after(acted, ("tok2", "kb")))
                for j in range(2):
                    turn_two(("kb", j), tok2, 2 * j)
                wide(u, 1, XT, 3, 4)
                u += 2
                wide(u, 0, XT, 0, 3)
                eng.wait_ge(acted, e.after(acted, ("tok2", "qb")))
                for j in range(2):
                    turn_two(("qb", j), tok2, 2 * j)
                eng.wait_ge(done, e.after(done, ("rope",)))
                turn_two(("qkt", 0), qkr, 0)
                turn_two(("qkt", 1), qkr, 2)
                wide(u, 0, XT, 3, 4)
                u += 2
                wide(u, 1, XT, 0, 1)
                turn_two(("qkt", 2), qkr, 4)
                wide(u, 1, XT, 1, 3)
                eng.wait_ge(acted, e.after(acted, ("qkt", 2)))
                for h in range(4):
                    score(h)
                wide(u, 1, XT, 3, 4)
                u += 2
                eng.wait_ge(acted, e.after(acted, ("vb", 0)))
                wide(u, 0, XT, 0, 1)
                for h in range(4, 8):
                    score(h)
                wide(u, 0, XT, 1, 3)
                eng.wait_ge(done, e.after(done, ("loga", 1)))
                exponents(0, 0)
                wide(u, 0, XT, 3, 4)
                exponents(0, 1)
                u += 2
                eng.wait_ge(acted, e.after(acted, ("vb", 1)))
                wide(u, 1, XT, 0, 3)
                eng.wait_ge(acted, e.after(acted, ("prob", 0)))
                prob_turn(0)
                prob_turn(1)
                wide(u, 1, XT, 3, 4)
                eng.wait_ge(acted, e.after(acted, ("prob", 1)))
                prob_turn(2)
                prob_turn(3)
                u += 2
                eng.wait_ge(acted, e.after(acted, ("rb", 0)))
                wide(u, 0, XT, 0, 1)
                weights(0, 0)
                weights(0, 1)
                prob_turn(4)
                wide(u, 0, XT, 1, 2)
                weights(0, 2)
                weights(0, 3)
                cross(0)
                prob_turn(5)
                wide(u, 0, XT, 2, 3)
                exponents(1, 0)
                eng.wait_ge(acted, e.after(acted, ("prob_t", 5)))
                attention(0)
                attention(1)
                wide(u, 0, XT, 3, 4)
                exponents(1, 1)
                u += 2
                eng.wait_ge(acted, e.after(acted, ("rb", 1)))
                wide(u, 1, XT, 0, 1)
                eng.wait_ge(done, e.after(done, ("oa", 1)))
                turn_two(("oat", 0), oa, 0)
                turn_two(("oat", 1), oa, 2)
                linear_out(0)
                wide(u, 1, XT, 1, 2)
                weights(1, 0)
                wide(u, 1, XT, 2, 3)
                weights(1, 1)
                wide(u, 1, XT, 3, 4)
                u += 2
                for op in [o for o in SMALL_OPS[:FOUR_BANKS] if BANK[o] in (4, 5)][-2:]:
                    reader = acted if op[0] in READ_BY_SCALAR else done
                    eng.wait_ge(reader, e.after(reader, op))
                eng.wait_ge(done, e.after(done, ("oat", 1)))
                blocks(u, 0, 2, OA, (0,), True, False, False)
                weights(1, 2)
                blocks(u, 1, 2, OA, (1,), False, False, True)
                weights(1, 3)
                cross(1)
                blocks(u + 1, 0, 2, OA, (2,), False, False, False)
                exponents(2, 0)
                blocks(u + 1, 1, 2, OA, (3,), False, True, True)
                exponents(2, 1)
                u += 2
                eng.wait_ge(acted, e.after(acted, ("sig", "a", 0)))
                blocks(u, 0, 0, OA, (0,), True, False, False)
                linear_out(1)
                blocks(u, 1, 0, OA, (1,), False, False, True)
                weights(2, 0)
                blocks(u + 1, 0, 0, OA, (2,), False, False, False)
                weights(2, 1)
                blocks(u + 1, 1, 0, OA, (3,), False, True, True)
                weights(2, 2)
                u += 2
                eng.wait_ge(acted, e.after(acted, ("sig", "a", 1)))
                wide(u, 1, XT, 0, 1)
                weights(2, 3)
                cross(2)
                exponents(3, 0)
                wide(u, 1, XT, 1, 2)
                exponents(3, 1)
                linear_out(2)
                wide(u, 1, XT, 2, 3)
                weights(3, 0)
                weights(3, 1)
                wide(u, 1, XT, 3, 4)
                weights(3, 2)
                weights(3, 3)
                cross(3)
                u += 2
                eng.wait_ge(done, e.after(done, ("merged", "a", 0)))
                wide(u, 2, XT, 0, 1)
                linear_out(3)
                wide(u, 2, XT, 1, 3)
                eng.wait_ge(done, e.after(done, ("obn",)))
                turn_two(("obt", 0), rb, 0)
                turn_two(("obt", 1), rb, 2)
                wide(u, 2, XT, 3, 4)
                u += 2
                eng.wait_ge(done, e.after(done, ("merged", "a", 1)))
                eng.wait_ge(done, e.after(done, ("obt", 1)))
                wide(u, 0, OB, 0, 1)
                turn_two(("obt", 2), rb, 4)
                turn_two(("obt", 3), rb, 6)
                wide(u, 0, OB, 1, 2)
                eng.wait_ge(done, e.after(done, ("obt", 3)))
                wide(u, 0, OB, 2, 4)
                u += 2
                eng.wait_ge(acted, e.after(acted, ("sig", "b", 0)))
                wide(u, 1, OB, 0, 2)
                eng.wait_ge(done, e.after(done, ("merged", "b", 0)))
                turn_two(("mt", 0, 0), merged2, 0)
                turn_two(("mt", 0, 1), merged2, 2)
                wide(u, 1, OB, 2, 4)
                u += 2
                eng.wait_ge(acted, e.after(acted, ("sig", "b", 1)))
                eng.wait_ge(done, e.after(done, ("mt", 0, 1)))
                wide(u, 2, MERGED, 0, 1)
                eng.wait_ge(done, e.after(done, ("merged", "b", 1)))
                turn_two(("mt", 1, 0), merged2, 4)
                turn_two(("mt", 1, 1), merged2, 6)
                wide(u, 2, MERGED, 1, 2)
                eng.wait_ge(done, e.after(done, ("mt", 1, 1)))
                wide(u, 2, MERGED, 2, 4)
                u += 2
                wide(u, 1, MERGED, 0, 1)
                eng.wait_ge(done, e.after(done, ("x", "ffn1", 0)))
                x_transposes("ffn1", 0)
                wide(u, 1, MERGED, 1, 4)
                assert u + 2 == u0 + MIX_UNITS[2]

            eng.wait_ge(consts_in, 16 * N_CONSTS)
            for b in (1, 2):
                nc.tensor.transpose(psum[:, 3 + b, 0:VR[b]], vrows[0:VR[b], b - 1, :],
                                    ident[0:VR[b], 0:VR[b]]).then_inc(small, e.mark(small, ("vecs", b)))
            x_transposes("ffn0", 0)
            eng.sem_inc(w_used, HL)
            with e.layers(1):
                ffn_tensor(0, 0, "mix")
                mix1_tensor(FFN_UNITS)
                ffn_tensor(FFN_UNITS + MIX_UNITS[1], 1, "ffn0")
            e.enter("between")
            eng.wait_ge(done, e.after(done, ("final", 0)))
            x_transposes("ffn0", 0)
            with e.layers(2):
                ffn_tensor(0, 0, "mix")
                mix2_tensor(FFN_UNITS)
                ffn_tensor(FFN_UNITS + MIX_UNITS[2], 1, "ffn0")
            e.enter("end")

        @block.scalar
        def _(eng):
            e = Engine(eng, counts, known, act_own)

            def split(u):
                eng.wait_ge(raw_in[u % RAW], loaded(e, u))
                eng.wait_ge(w_used, units(e, u))
                n = SHORT.get(e.segment, {}).get(u, 2048)
                nc.scalar.activation(whi[:, u % HL, 0:n], raw[:, u % RAW, 0:n], ACT.Copy).then_inc(hi_done, 1)

            def multiplied(u):
                eng.wait_ge(w_used, units(e, u, HL))

            def turned_hi(hi, label, bank, first, gain=None):
                eng.wait_ge(small, e.after(small, label))
                if gain is None:
                    last = nc.scalar.activation(hi[:, first:first + 2, :], psum[:, bank, :], ACT.Copy)
                else:
                    for i in range(2):
                        last = nc.scalar.activation(hi[:, first + i, :], psum[:, bank, i * T:(i + 1) * T], ACT.Copy,
                                                    scale=v[:, gain + i:gain + i + 1])
                last.then_inc(acted, e.mark(acted, label))

            def x_hi(stage, half):
                for j in range(2):
                    turned_hi(xt_hi, ("xt", stage, half, j), 6 + j, 4 * half + 2 * j, V_GAIN[stage] + 4 * half + 2 * j)

            def squares(stage, out):
                for m in range(MT):
                    last = nc.scalar.activation(out[m], x[:, m, :], ACT.Square, accum_out=ss[:, m:m + 1])
                last.then_inc(acted, e.mark(acted, ("ss", stage)))

            def root(stage):
                eng.wait_ge(done, e.after(done, ("ms", stage)))
                nc.scalar.activation(rt[:, :], ms[:, :], ACT.Sqrt).then_inc(acted, e.mark(acted, ("rt", stage)))

            def stage_start(stage, u0, out):
                squares(stage, out)
                root(stage)
                split(u0 + 3)
                if stage == "mix":
                    split(u0 + 4)
                eng.wait_ge(done, e.after(done, ("rstd", stage)))

            def ffn_scalar(u0, f, next_stage):
                stage = f"ffn{f}"

                def gates(g):
                    multiplied(u0 + 2 * g + 1)
                    eng.wait_ge(hid_done, groups(e, f, g - 1, 2))
                    for m in range(MT):
                        last = nc.scalar.activation(gate[:, m, :], psum[:, 2 * (g % 2) + m, 0:256], ACT.Silu,
                                                    scale=rstd[:, m:m + 1])
                        last.then_inc(gate_done, 1)

                def hidden_hi(g, chunk):
                    eng.wait_ge(ht_ready, groups(e, f, g))
                    nc.scalar.activation(ht_hi[:, chunk, :], psum[:, 6 + g % 2, :], ACT.Copy).then_inc(ht_hi_done, 1)

                x_hi(stage, 1)
                stage_start(stage, u0, [junk[:, m, :] for m in range(MT)])
                with e.turns((FG - 1) // 2):
                    for g in range(2):
                        gates(g)
                        split(u0 + 2 * g + 4)
                        hidden_hi(g, bass.ds(e.it * 4 + 2 * g, 2))
                        split(u0 + 2 * g + 5)
                g = FG - 1
                gates(g)
                split(u0 + 2 * g + 4)
                hidden_hi(g, slice(2 * g, 2 * g + 2))
                split(u0 + 2 * g + 5)
                for s in range(2 * FG + 1, FFN_UNITS):
                    if s == 2 * FG + 6:
                        if next_stage == "ffn0":
                            eng.wait_ge(done, e.after(done, ("v",)))
                        x_hi(next_stage, 0)
                    split(u0 + s + 3)

            def mix1_scalar(u0):
                def to_sbuf(label, out, p, u):
                    multiplied(u)
                    for m in range(MT):
                        last = nc.scalar.activation(out[:, m, :], psum[:, 2 * p + m, :], ACT.Copy,
                                                    scale=rstd[:, m:m + 1])
                    last.then_inc(acted, e.mark(acted, label))

                multiplied(u0 - 1)
                eng.dma_start(cs[:, :, :], a["t_cs"].rearrange("(m p) n -> p m n", p=P)).then_inc(mix_in, 16)
                eng.dma_start(cc[:, :], a["t_cc"]).then_inc(mix_in, 16)
                eng.dma_start(poolm[:, :, :, :], a["t_pool"].rearrange("(m p) (g t) -> p m g t", p=P, g=4)
                              ).then_inc(mix_in, 16)
                eng.dma_start(pscale[:, :], a["pool_scale"][bass.ds(e.lay, 1), :].partition_broadcast(P)
                              ).then_inc(mix_in, 16)
                x_hi("mix", 1)
                stage_start("mix", u0, [w[:, :, :].rearrange("p m n -> p (m n)") for w in (z, cv)])
                to_sbuf(("tok", "F"), tok, 0, u0 + 1)
                split(u0 + 5)
                for g in (0, 1):
                    eng.wait_ge(small, e.after(small, ("ab", g)))
                    nc.scalar.activation(ab[:, g, :], psum[:, 6 + g % 2, :], ACT.Copy).then_inc(
                        acted, e.mark(acted, ("ab", g)))
                split(u0 + 6)
                for g in (2, 3):
                    eng.wait_ge(small, e.after(small, ("ab", g)))
                    nc.scalar.activation(ab[:, g, :], psum[:, 6 + g % 2, :], ACT.Copy).then_inc(
                        acted, e.mark(acted, ("ab", g)))
                to_sbuf(("tok", "P"), ptok, 1, u0 + 3)
                split(u0 + 7)
                for j in range(2):
                    turned_hi(fq_hi, ("fq", j), 6 + j, 2 * j)
                split(u0 + 8)
                for j in range(2):
                    turned_hi(pl_hi, ("pl", j), 6 + j, 2 * j)
                to_sbuf(("tok", "C"), z, 0, u0 + 5)
                split(u0 + 9)
                split(u0 + 10)
                split(u0 + 11)
                for j in range(2):
                    eng.wait_ge(small, e.after(small, ("zt", j)))
                    nc.scalar.activation(zt[:, 2 * j:2 * j + 2, 1:T + 1],
                                               psum[:, 6 + j, :].rearrange("p (c t) -> p c t", c=2), ACT.Copy).then_inc(
                                                   acted, e.mark(acted, ("zt", j)))
                split(u0 + 12)
                to_sbuf(("tok", "B"), tok, 0, u0 + 9)
                split(u0 + 13)
                for j in range(2):
                    eng.wait_ge(done, e.after(done, ("bc", j)))
                    nc.scalar.activation(bz_hi[:, 2 * j:2 * j + 2, :], cv[:, 2 * j:2 * j + 2, :], ACT.Copy).then_inc(
                        acted, e.mark(acted, ("bz", j)))
                split(u0 + 14)
                s = 12
                for n in range(2):
                    for b, branch in enumerate(("f", "p", "c")):
                        multiplied(u0 + s - 1)
                        if (n, b) != (0, 0):
                            eng.wait_ge(done, e.after(done, ("merged", n - (b == 0), ("c", "f", "p")[b])))
                        for m in range(MT):
                            last = nc.scalar.activation(sig1[:, m, :], psum[:, 2 * ((1 + b + n) % 2) + m, :],
                                                        ACT.Sigmoid, scale=rstd[:, m:m + 1])
                        last.then_inc(acted, e.mark(acted, ("sig", n, branch)))
                        split(u0 + s + 3)
                        if (n, b) != (1, 2):
                            split(u0 + s + 4)
                        if (n, b) == (1, 0):
                            for j in range(2):
                                turned_hi(mt1_hi, ("mt0", j), 6 + j, 2 * j)
                        if s + 5 < 31:
                            split(u0 + s + 5)
                        s += 3
                for j in range(2):
                    turned_hi(mt1_hi, ("mt1", j), 6 + j, 4 + 2 * j)
                split(u0 + 31)
                split(u0 + 32)
                x_hi("ffn1", 0)
                split(u0 + 33)
                split(u0 + 34)

            def mix2_scalar(u0):
                def bank(label):
                    eng.wait_ge(small, e.after(small, label))
                    return psum[:, BANK[label], :]

                def copied(label, out, src, scale=1.0, func=ACT.Copy):
                    nc.scalar.activation(out, src, func, scale=scale).then_inc(acted, e.mark(acted, label))

                def projected(label, u, parts):
                    multiplied(u)
                    for m in range(MT):
                        for out, src in parts(m):
                            last = nc.scalar.activation(out, src, ACT.Copy, scale=rstd[:, m:m + 1])
                    last.then_inc(acted, e.mark(acted, label))

                def two(w):
                    return w.rearrange("p (c t) -> p c t", c=2)

                def decay(m):
                    src = bank(("loga", m))
                    out = softplus[:, m, :]
                    e.link(nc.scalar.activation(out, src, ACT.Abs))
                    e.link(nc.scalar.activation(out, out, ACT.Exp, scale=-1.0))
                    nc.scalar.activation(out, out, ACT.Ln, bias=1.0).then_inc(acted, e.mark(acted, ("softplus", m)))

                def exponentials(hh):
                    eng.wait_ge(done, e.after(done, ("nm", hh)))
                    for h in range(4 * hh, 4 * hh + 4):
                        for b, blocks in enumerate((slice(0, 1), slice(1, 3))):
                            part = prob[:, h, blocks, :]
                            nc.scalar.activation(part, part, ACT.Exp, bias=nm[:, h, b:b + 1],
                                                 accum_out=rs[:, h, b:b + 1])
                    part = dm[:, 4 * hh:4 * hh + 4, :]
                    nc.scalar.activation(part, part, ACT.Exp).then_inc(acted, e.mark(acted, ("prob", hh)))

                def prob_turned(j):
                    copied(("prob_t", j), prob_t[:, 4 * j:4 * j + 4, :],
                           bank(("prob_t", j)).rearrange("p (b t) -> p b t", b=4))

                def decays(h, part):
                    if h >= 2:
                        eng.wait_ge(small, e.after(small, ("cross", h - 2)))
                    for m in range(MT):
                        copied(("ex", h, part, m), xg[:, h % 2, 4 * part:4 * part + 4, m * P:(m + 1) * P],
                               bank(("ex", h, part, m)).rearrange("p (l t) -> p l t", l=4), func=ACT.Exp)

                def cross(h):
                    if h:
                        eng.wait_ge(small, e.after(small, ("ob", h - 1)))
                    copied(("cross", h), px[:, :], bank(("cross", h))[:, 0:P])

                def out_squares(h):
                    if h:
                        eng.wait_ge(acted, e.after(acted, ("so", h - 1)))
                    src = bank(("ob", h))
                    for m in range(MT):
                        last = nc.scalar.activation(so_junk[:, :], src[:, m * DV:(m + 1) * DV], ACT.Square,
                                                    accum_out=so[:, 0, 2 * h + m:2 * h + m + 1])
                        if m == 0:
                            e.link(last)
                    last.then_inc(acted, e.mark(acted, ("so", h)))

                def hi_turned(hi, label, first, gain=None):
                    bank(label)
                    turned_hi(hi, label, BANK[label], first, gain)

                def sigmoids(branch, n, p, u):
                    multiplied(u)
                    if branch == "b":
                        eng.wait_ge(done, e.after(done, ("merged", "a", n)))
                    for m in range(MT):
                        last = nc.scalar.activation(sig2[:, m, 512 * n:512 * n + 512], psum[:, 2 * p + m, :],
                                                    ACT.Sigmoid, scale=rstd[:, m:m + 1])
                    last.then_inc(acted, e.mark(acted, ("sig", branch, n)))

                x_hi("mix", 1)
                lay = bass.ds(e.lay, 1)

                def table(out, src):
                    eng.dma_start(out, src).then_inc(mix_in, 16)
                table(spans[:, :, :], a["t_spans"].rearrange("p (a n) -> p a n", a=3))
                table(pairs[:, :, :], a["t_pairs"].rearrange("p (a n) -> p a n", a=LEVELS))
                table(window[:, :], a["t_window"])
                table(rope[:, :, :, :], a["t_rope"].rearrange("(m p) (a n) -> p m a n", p=P, a=2))
                table(qk_gain[:, 0, :], a["swa_q_norm_2"][lay, :].partition_broadcast(P))
                table(qk_gain[:, 1, :], a["swa_k_norm_2"][lay, :].partition_broadcast(P))
                table(sinks[:, :], a["swa_sinks_2"][lay, :].partition_broadcast(P))
                table(gwb[0:RANK, :], a["gla_w_gate_2"].rearrange("l r n -> (l r) n")[bass.ds(e.lay * RANK, RANK), :])
                table(gwb[RANK:RANK + 1, :], a["gla_gate_bias_2"][lay, :])
                stage_start("mix", u0, [w[:, :, :].rearrange("p m n -> p (m n)") for w in (tok2, loga)])
                projected(("qa",), u0 + 1, lambda m: [(qk[:, m, 0:512], psum[:, m, :])])
                split(u0 + 5)
                projected(("kv",), u0 + 2, lambda m: [
                    (qk[:, m, 512:QK].rearrange("p (h two d) -> p h two d", h=2, two=2),
                     psum[:, 2 + m, 0:P].rearrange("p (h two d) -> p h two d", h=2, two=1)
                     .broadcast_to([P, 2, 2, HEAD_DIM])),
                    (va[:, m, :], psum[:, 2 + m, P:2 * P])])
                split(u0 + 6)
                eng.wait_ge(done, e.after(done, ("glt1",)))
                projected(("gl",), u0 + 3, lambda m: [(gl[:, m, :], psum[:, 4 + m, 0:RANK])])
                eng.wait_ge(done, e.after(done, ("s24",)))
                nc.scalar.activation(s24[:, 2, :], s24[:, 1, :], ACT.Sqrt).then_inc(acted, e.mark(acted, ("s24",)))
                split(u0 + 7)
                copied(("glt",), glt[0:RANK, :], bank(("glt",))[0:RANK, 0:T])
                split(u0 + 8)
                projected(("tok2", "kb"), u0 + 5, lambda m: [(tok2[:, m, :], psum[:, m, :])])
                decay(0)
                split(u0 + 9)
                decay(1)
                for j in range(2):
                    copied(("kb", j), kbt[:, 2 * j:2 * j + 2, :], two(bank(("kb", j))))
                split(u0 + 10)
                projected(("tok2", "qb"), u0 + 7, lambda m: [(tok2[:, m, :], psum[:, 2 + m, :])])
                split(u0 + 11)
                for j in range(2):
                    copied(("qb", j), qbt[:, 2 * j:2 * j + 2, :], two(bank(("qb", j))), scale=DK ** -0.5)

                def qk_turned(j):
                    copied(("qkt", j), qkt[:, 2 * j:2 * j + 2, :], two(bank(("qkt", j))))
                qk_turned(0)
                qk_turned(1)
                split(u0 + 12)
                qk_turned(2)
                projected(("vb", 0), u0 + 9, lambda m: [(vb[:, m, 0:512], psum[:, m, :])])
                split(u0 + 13)
                split(u0 + 14)
                projected(("vb", 1), u0 + 11, lambda m: [(vb[:, m, 512:D], psum[:, 2 + m, :])])
                exponentials(0)
                split(u0 + 15)
                decays(0, 0)
                exponentials(1)
                split(u0 + 16)
                decays(0, 1)
                projected(("rb", 0), u0 + 13, lambda m: [(rb[:, m, 0:512], psum[:, m, :])])
                split(u0 + 17)
                for j in range(4):
                    prob_turned(j)
                split(u0 + 18)
                projected(("rb", 1), u0 + 15, lambda m: [(rb[:, m, 512:D], psum[:, 2 + m, :])])
                prob_turned(4)
                split(u0 + 19)
                cross(0)
                prob_turned(5)
                split(u0 + 20)
                decays(1, 0)
                decays(1, 1)
                sigmoids("a", 0, 0, u0 + 17)
                split(u0 + 21)
                for m in range(MT):
                    last = nc.scalar.activation(rb[:, m, :], rb[:, m, :], ACT.Silu)
                last.then_inc(acted, e.mark(acted, ("silu",)))
                for j in range(2):
                    hi_turned(oa_hi, ("oat", j), 2 * j)
                out_squares(0)
                split(u0 + 22)
                sigmoids("a", 1, 1, u0 + 19)
                split(u0 + 23)
                cross(1)
                decays(2, 0)
                split(u0 + 24)
                decays(2, 1)
                out_squares(1)
                split(u0 + 25)
                split(u0 + 26)
                cross(2)
                decays(3, 0)
                split(u0 + 27)
                decays(3, 1)
                out_squares(2)
                split(u0 + 28)
                cross(3)
                out_squares(3)
                eng.wait_ge(done, e.after(done, ("so",)))
                nc.scalar.activation(so[:, 2, :], so[:, 1, :], ACT.Sqrt).then_inc(acted, e.mark(acted, ("so_root",)))
                split(u0 + 29)
                for j in range(2):
                    hi_turned(ob_hi, ("obt", j), 2 * j, V_OUT_NORM + 2 * j)
                sigmoids("b", 0, 1, u0 + 25)
                split(u0 + 30)
                for j in (2, 3):
                    hi_turned(ob_hi, ("obt", j), 2 * j, V_OUT_NORM + 2 * j)
                split(u0 + 31)
                sigmoids("b", 1, 2, u0 + 27)
                split(u0 + 32)
                split(u0 + 33)
                for j in range(2):
                    hi_turned(mt2_hi, ("mt", 0, j), 2 * j)
                split(u0 + 34)
                for j in range(2):
                    hi_turned(mt2_hi, ("mt", 1, j), 4 + 2 * j)
                split(u0 + 35)
                split(u0 + 36)
                x_hi("ffn1", 0)
                split(u0 + 37)
                split(u0 + 38)

            eng.wait_ge(done, e.after(done, ("v",)))
            x_hi("ffn0", 0)
            for u in range(3):
                split(u)
            with e.layers(1):
                ffn_scalar(0, 0, "mix")
                mix1_scalar(FFN_UNITS)
                ffn_scalar(FFN_UNITS + MIX_UNITS[1], 1, "ffn0")
            e.enter("between")
            eng.wait_ge(x_whole, wholes(e))
            eng.dma_start(gfin[:, :], a["g_final"].rearrange("(a n) -> a n", a=1).partition_broadcast(P)
                          ).then_inc(gfin_in, 16)
            squares("final", [junk[:, m, :] for m in range(MT)])
            root("final")
            x_hi("ffn0", 0)
            with e.layers(2):
                ffn_scalar(0, 0, "mix")
                mix2_scalar(FFN_UNITS)
                ffn_scalar(FFN_UNITS + MIX_UNITS[2], 1, "ffn0")
            e.enter("end")

        @block.vector
        def _(eng):
            e = Engine(eng, counts, known, dve_own)

            def split(u):
                eng.wait_ge(hi_done, units(e, u))
                n = SHORT.get(e.segment, {}).get(u, 2048)
                nc.vector.tensor_tensor(wlo[:, u % HL, 0:n], raw[:, u % RAW, 0:n], whi[:, u % HL, 0:n],
                                        ALU.subtract).then_inc(w_ready, 1)

            def multiplied(u):
                eng.wait_ge(w_used, units(e, u, HL))

            def turned_lo(hi, lo, label, bank, first, gain=None):
                eng.wait_ge(acted, e.after(acted, label))
                if gain is None:
                    last = nc.vector.tensor_tensor(lo[:, first:first + 2, :],
                                                   psum[:, bank, :].rearrange("p (c t) -> p c t", c=2),
                                                   hi[:, first:first + 2, :], ALU.subtract)
                else:
                    for i in range(2):
                        last = nc.vector.scalar_tensor_tensor(
                            out=lo[:, first + i, :], in0=psum[:, bank, i * T:(i + 1) * T],
                            scalar=v[:, gain + i:gain + i + 1], in1=hi[:, first + i, :].bitcast(F32),
                            op0=ALU.mult, op1=ALU.subtract)
                last.then_inc(done, e.mark(done, label))

            def x_lo(stage, half):
                for j in range(2):
                    turned_lo(xt_hi, xt_lo, ("xt", stage, half, j), 6 + j, 4 * half + 2 * j,
                              V_GAIN[stage] + 4 * half + 2 * j)

            def half_done():
                eng.wait_ge(done, e.after(done, ("xt", "ffn0", 0, 1)))
                eng.sem_inc(x_half, 1)

            def add_to_x(p, half, factor):
                for m in range(MT):
                    part = x[:, m, 512 * half:512 * half + 512]
                    last = nc.vector.scalar_tensor_tensor(out=part, in0=psum[:, 2 * p + m, :], scalar=factor,
                                                          in1=part, op0=ALU.mult, op1=ALU.add)
                return last

            def norm(stage):
                eng.wait_ge(acted, e.after(acted, ("ss", stage)))
                nc.vector.tensor_scalar(ms[:, :], ss[:, :], 1.0 / D, EPS, ALU.mult, ALU.add).then_inc(
                    done, e.mark(done, ("ms", stage)))
                eng.wait_ge(acted, e.after(acted, ("rt", stage)))
                e.link(nc.vector.reciprocal(nt[:, 0, :], rt[:, :]))
                rsqrt_newton(rstd[:, :], ms[:, :], nt[:, 0, :], nt[:, 1, :], ("rstd", stage))

            def rsqrt_newton(out, value, r, t, label):
                e.link(nc.vector.tensor_tensor(t, r, r, ALU.mult))
                e.link(nc.vector.tensor_tensor(t, t, value, ALU.mult))
                e.link(nc.vector.tensor_scalar(t, t, -0.5, 1.5, ALU.mult, ALU.add))
                ins = nc.vector.tensor_tensor(out, r, t, ALU.mult)
                ins.then_inc(done, e.mark(done, label))
                eng.wait_ge(done, e.after(done, label))

            def small_vectors(first, n):
                nc.vector.tensor_copy(v[:, 0:n], vecs[:, bass.ds(first, n)]).then_inc(done, e.mark(done, ("v",)))
                eng.wait_ge(done, e.after(done, ("v",)))

            def stage_start(stage, u0, p, factor):
                if stage != "ffn0":
                    multiplied(u0 - 1)
                    add_to_x(p, 1, factor).then_inc(done, e.mark(done, ("x", stage, 1)))
                split(u0 + 2)
                x_lo(stage, 1)
                norm(stage)
                split(u0 + 3)
                if stage == "mix":
                    split(u0 + 4)

            def ffn_vector(u0, f, next_stage):
                stage = f"ffn{f}"

                def hidden(g):
                    if (f, g) == (0, 0):
                        eng.wait_ge(ht_done, groups(e, f, g - 1, 2))
                    else:
                        eng.wait_ge(ht_ready, groups(e, f, g - 1))
                    for m in range(MT):
                        eng.wait_ge(gate_done, gates(e, f, g, m))
                        last = nc.vector.scalar_tensor_tensor(
                            out=hid[:, m, :], in0=psum[:, 2 * (g % 2) + m, 256:512], scalar=rstd[:, m:m + 1],
                            in1=gate[:, m, :], op0=ALU.mult, op1=ALU.mult)
                    last.then_inc(hid_done, 1)

                def hidden_lo(g, chunk):
                    eng.wait_ge(ht_hi_done, groups(e, f, g))
                    nc.vector.tensor_tensor(ht_lo[:, chunk, :],
                                            psum[:, 6 + g % 2, :].rearrange("p (c t) -> p c t", c=2),
                                            ht_hi[:, chunk, :], ALU.subtract).then_inc(ht_done, 1)

                stage_start(stage, u0, 1, 1.0)
                with e.turns((FG - 1) // 2):
                    for g in range(2):
                        hidden(g)
                        split(u0 + 2 * g + 4)
                        hidden_lo(g, bass.ds(e.it * 4 + 2 * g, 2))
                        split(u0 + 2 * g + 5)
                g = FG - 1
                hidden(g)
                split(u0 + 2 * g + 4)
                hidden_lo(g, slice(2 * g, 2 * g + 2))
                split(u0 + 2 * g + 5)
                for s in range(2 * FG + 1, FFN_UNITS - 1):
                    if s == 2 * FG + 5:
                        multiplied(u0 + s)
                        add_to_x(2, 0, 0.5).then_inc(done, e.mark(done, ("x", next_stage, 0)))
                    if s == 2 * FG + 6:
                        if next_stage == "ffn0":
                            per = VR[e.segment] // LAYERS
                            small_vectors({1: 0, 2: VR[1]}[e.segment] + per + e.lay * per, per)
                        x_lo(next_stage, 0)
                        if next_stage == "ffn0":
                            half_done()
                    split(u0 + s + 3)
                if next_stage == "ffn0":
                    multiplied(u0 + FFN_UNITS - 1)
                    add_to_x(1, 1, 0.5).then_inc(x_whole, 1)

            def mix1_vector(u0):
                stage_start("mix", u0, 1, 0.5)
                split(u0 + 5)
                split(u0 + 6)
                split(u0 + 7)
                for j in range(2):
                    turned_lo(fq_hi, fq_lo, ("fq", j), 6 + j, 2 * j)
                split(u0 + 8)
                for j in range(2):
                    turned_lo(pl_hi, pl_lo, ("pl", j), 6 + j, 2 * j)
                split(u0 + 9)
                split(u0 + 10)
                eng.wait_ge(acted, e.after(acted, ("tok", "C")))
                multiplied(u0 + 7)
                for m in range(MT):
                    ins = nc.vector.scalar_tensor_tensor(out=z[:, m, :], in0=psum[:, 2 + m, :],
                                                         scalar=rstd[:, m:m + 1], in1=z[:, m, :],
                                                         op0=ALU.mult, op1=ALU.mult)
                    ins.then_inc(done, e.mark(done, ("z", m)))
                e.link(nc.vector.memset(zt[:, :, 0:1], 0.0))
                e.link(nc.vector.memset(zt[:, :, T + 1:T + 2], 0.0))
                split(u0 + 11)
                for j in range(2):
                    eng.wait_ge(acted, e.after(acted, ("zt", j)))
                    for tap, first in ((1, True), (0, False), (2, False)):
                        for c in (2 * j, 2 * j + 1):
                            w = v[:, V_CONV + 4 * tap + c:V_CONV + 4 * tap + c + 1]
                            src = zt[:, c, tap:tap + T]
                            if first:
                                ins = nc.vector.tensor_scalar(cv[:, c, :], src, w, None, ALU.mult)
                            else:
                                ins = nc.vector.scalar_tensor_tensor(out=cv[:, c, :], in0=src, scalar=w,
                                                                     in1=cv[:, c, :], op0=ALU.mult, op1=ALU.add)
                        e.link(ins)
                split(u0 + 12)
                split(u0 + 13)
                for j in range(2):
                    eng.wait_ge(small, e.after(small, ("bt", j)))
                    nc.vector.tensor_tensor(cv[:, 2 * j:2 * j + 2, :],
                                                  psum[:, 6 + j, :].rearrange("p (c t) -> p c t", c=2),
                                                  cv[:, 2 * j:2 * j + 2, :], ALU.mult).then_inc(
                                                      done, e.mark(done, ("bc", j)))
                for j in range(2):
                    eng.wait_ge(acted, e.after(acted, ("bz", j)))
                    nc.vector.tensor_tensor(bz_lo[:, 2 * j:2 * j + 2, :], cv[:, 2 * j:2 * j + 2, :],
                                                  bz_hi[:, 2 * j:2 * j + 2, :], ALU.subtract).then_inc(
                                                      done, e.mark(done, ("bz", j)))
                split(u0 + 14)
                s = 12
                for n in range(2):
                    for b, branch in enumerate(("f", "p", "c")):
                        if (n, b) != (1, 2):
                            split(u0 + s + 3)
                        multiplied(u0 + s)
                        eng.wait_ge(acted, e.after(acted, ("sig", n, branch)))
                        if (n, b) == (1, 0):
                            eng.wait_ge(small, e.after(small, ("mt0", 1)))
                        for m in range(MT):
                            y = psum[:, 4 + m, :]
                            if b == 0:
                                ins = nc.vector.tensor_tensor(merged1[:, m, :], y, sig1[:, m, :], ALU.mult)
                            else:
                                e.link(nc.vector.tensor_tensor(part1[:, :], y, sig1[:, m, :], ALU.mult))
                                if b == 1:
                                    e.link(nc.vector.tensor_tensor(part1[:, :], part1[:, :],
                                                                   pscale[:, 512 * n:512 * n + 512], ALU.mult))
                                ins = nc.vector.tensor_tensor(merged1[:, m, :], merged1[:, m, :], part1[:, :], ALU.add)
                            if m == 0:
                                e.link(ins)
                        ins.then_inc(done, e.mark(done, ("merged", n, branch)))
                        eng.wait_ge(done, e.after(done, ("merged", n, branch)))
                        split(u0 + s + (3 if (n, b) == (1, 2) else 4))
                        if (n, b) == (1, 0):
                            for j in range(2):
                                turned_lo(mt1_hi, mt1_lo, ("mt0", j), 6 + j, 2 * j)
                        if s + 5 < 31:
                            split(u0 + s + 5)
                        s += 3
                for j in range(2):
                    turned_lo(mt1_hi, mt1_lo, ("mt1", j), 6 + j, 4 + 2 * j)
                split(u0 + 31)
                split(u0 + 32)
                multiplied(u0 + 29)
                add_to_x(0, 0, 1.0).then_inc(done, e.mark(done, ("x", "ffn1", 0)))
                x_lo("ffn1", 0)
                split(u0 + 33)

            def mix2_vector(u0):
                def bank(label):
                    return psum[:, BANK[label], :]

                def heads(w, n):
                    return w.rearrange("p m (h d) -> p m h d", h=n)

                def score(h):
                    eng.wait_ge(small, e.after(small, ("score", h)))
                    ins = nc.vector.scalar_tensor_tensor(
                        out=prob[:, h, :, :].rearrange("p b t -> p (b t)"), in0=bank(("score", h))[:, 0:3 * P],
                        scalar=HEAD_DIM ** -0.5, in1=window[:, :], op0=ALU.mult, op1=ALU.add)
                    ins.then_inc(done, e.mark(done, ("score", h)))
                    eng.wait_ge(done, e.after(done, ("score", h)))
                    nc.vector.tensor_reduce(mx[:, h, 0:1], prob[:, h, 0, :], axis=AX_X, op=ALU.max)
                    return nc.vector.tensor_reduce(mx[:, h, 1:2],
                                                   prob[:, h, 1:3, :].rearrange("p b t -> p (b t)"),
                                                   axis=AX_X, op=ALU.max)

                def maxima(hh):
                    part = slice(4 * hh, 4 * hh + 4)
                    sink = sinks[:, part].unsqueeze(2).to_broadcast([P, 4, 2])
                    e.link(nc.vector.tensor_tensor(mx[:, part, :], mx[:, part, :], sink, ALU.max))
                    e.link(nc.vector.tensor_scalar(nm[:, part, :], mx[:, part, :], -1.0, None, ALU.mult))
                    nc.vector.tensor_tensor(dm[:, part, :], sink, mx[:, part, :], ALU.subtract).then_inc(
                        done, e.mark(done, ("nm", hh)))

                def decayed(h, part):
                    eng.wait_ge(acted, e.after(acted, ("ex", h, part, 1)))
                    for lv in range(4 * part, 4 * part + 4):
                        n = 1 << lv
                        for w, t in ((kbt, slice(0, n)), (qbt, slice(n, 2 * n))):
                            x_v = xg[:, h % 2, lv, :].rearrange("p (j w) -> p j w", w=2 * n)[:, :, t]
                            w_v = w[:, h, :].rearrange("p (j w) -> p j w", w=2 * n)[:, :, t]
                            ins = nc.vector.tensor_tensor(x_v, x_v, w_v, ALU.mult)
                    ins.then_inc(done, e.mark(done, ("decayed", h, part)))

                def weights(h, i):
                    if i == 0 and h:
                        eng.wait_ge(small, e.after(small, ("ob", h - 1)))
                    eng.wait_ge(small, e.after(small, ("weights", h, i)))

                    def level(k, n=1):
                        return bank(("weights", h, i))[:, 2 * k * P:2 * (k + n) * P].rearrange(
                            "p (l m t) -> p l m t", l=n, m=MT)

                    def mask(k, n=1):
                        lv = 2 * i + k
                        return pairs[:, lv:lv + n, :].rearrange("p l (o t) -> p l o t", o=1).broadcast_to([P, n, MT, P])
                    pg_v = pg[:, :, :].rearrange("p (l m) t -> p l m t", l=1)
                    if i == 0:
                        nc.vector.tensor_tensor(pg_v, level(0), mask(0), ALU.mult)
                        e.link(nc.vector.tensor_tensor(level(1), level(1), mask(1), ALU.mult))
                    else:
                        e.link(nc.vector.tensor_tensor(level(0, 2), level(0, 2), mask(0, 2), ALU.mult))
                        e.link(nc.vector.tensor_tensor(pg_v, pg_v, level(0), ALU.add))
                    nc.vector.tensor_tensor(pg_v, pg_v, level(1), ALU.add).then_inc(
                        done, e.mark(done, ("weights", h, i)))
                    eng.wait_ge(done, e.after(done, ("weights", h, i)))

                def gated(h):
                    eng.wait_ge(acted, e.after(acted, ("so", h)))
                    eng.wait_ge(acted, e.after(acted, ("silu",)))
                    for m in range(MT):
                        part = rb[:, m, h * DV:(h + 1) * DV]
                        ins = nc.vector.tensor_tensor(part, bank(("ob", h))[:, m * DV:(m + 1) * DV], part, ALU.mult)
                    ins.then_inc(done, e.mark(done, ("ob", h)))

                def merge(branch, n, p, u):
                    multiplied(u)
                    eng.wait_ge(acted, e.after(acted, ("sig", branch, n)))
                    cols = slice(512 * n, 512 * n + 512)
                    for m in range(MT):
                        y = psum[:, 2 * p + m, :]
                        if branch == "a":
                            ins = nc.vector.tensor_tensor(merged2[:, m, cols], y, sig2[:, m, cols], ALU.mult)
                        else:
                            e.link(nc.vector.tensor_tensor(part2[:, m, :], y, sig2[:, m, cols], ALU.mult))
                            ins = nc.vector.tensor_tensor(merged2[:, m, cols], merged2[:, m, cols], part2[:, m, :],
                                                          ALU.add)
                    ins.then_inc(done, e.mark(done, ("merged", branch, n)))

                def lo_turned(hi, lo, label, first, gain=None):
                    turned_lo(hi, lo, label, BANK[label], first, gain)

                stage_start("mix", u0, 1, 0.5)
                split(u0 + 5)
                nc.vector.memset(glt[0:32, :], 1.0).then_inc(done, e.mark(done, ("glt1",)))
                split(u0 + 6)
                eng.wait_ge(acted, e.after(acted, ("kv",)))
                e.link(nc.vector.tensor_tensor(qkr[:, :, :], qk[:, :, :], qk[:, :, :], ALU.mult))
                e.link(nc.vector.tensor_reduce(s24[:, 0, :], qkr[:, :, :].rearrange("p m (h d) -> p (m h) d", h=QK_HEADS),
                                               axis=AX_X, op=ALU.add))
                nc.vector.tensor_scalar(s24[:, 1, :], s24[:, 0, :], 1.0 / HEAD_DIM, EPS, ALU.mult, ALU.add).then_inc(
                    done, e.mark(done, ("s24",)))
                split(u0 + 7)
                eng.wait_ge(acted, e.after(acted, ("s24",)))
                e.link(nc.vector.reciprocal(s24[:, 2, :], s24[:, 2, :]))
                rsqrt_newton(s24[:, 0, :], s24[:, 1, :], s24[:, 2, :], s24[:, 3, :], ("r24",))
                e.link(nc.vector.tensor_tensor(
                    qkr[:, :, :].rearrange("p m (h d) -> p (m h) d", h=QK_HEADS),
                    qk[:, :, :].rearrange("p m (h d) -> p (m h) d", h=QK_HEADS),
                    s24[:, 0, :].unsqueeze(2).to_broadcast([P, MT * QK_HEADS, HEAD_DIM]), ALU.mult))
                split(u0 + 8)
                eng.wait_ge(mix_in, mix_tables(e))
                for m in range(MT):
                    for i, hs in enumerate((slice(0, HEADS), slice(HEADS, QK_HEADS))):
                        part = qkr[:, m, :].rearrange("p (h d) -> p h d", h=QK_HEADS)[:, hs, :]
                        ins = nc.vector.tensor_tensor(
                            part, part, qk_gain[:, i:i + 1, :].broadcast_to([P, hs.stop - hs.start, HEAD_DIM]),
                            ALU.mult)
                e.link(ins)
                split(u0 + 9)
                for m in range(MT):
                    eng.wait_ge(acted, e.after(acted, ("softplus", m)))
                    nc.vector.scalar_tensor_tensor(
                        out=loga[:, m, :], in0=bank(("loga", m)), scalar=0.0, in1=softplus[:, m, :],
                        op0=ALU.min, op1=ALU.subtract).then_inc(done, e.mark(done, ("loga", m)))
                for m in range(MT):
                    x_h = qkr[:, m, :].rearrange("p (h d) -> p h d", h=QK_HEADS)
                    o_h = qk[:, m, :].rearrange("p (h d) -> p h d", h=QK_HEADS)
                    x1, x2 = x_h[:, :, 0:32], x_h[:, :, 32:64]
                    cos, sin = (rope[:, m, i:i + 1, :].broadcast_to([P, QK_HEADS, 32]) for i in range(2))
                    ta, tb = (rope_t[:, i, :].rearrange("p (h d) -> p h d", h=QK_HEADS) for i in range(2))
                    nc.vector.tensor_tensor(o_h[:, :, 0:32], x1, cos, ALU.mult)
                    nc.vector.tensor_tensor(o_h[:, :, 32:64], x2, cos, ALU.mult)
                    nc.vector.tensor_tensor(ta, x2, sin, ALU.mult)
                    e.link(nc.vector.tensor_tensor(tb, x1, sin, ALU.mult))
                    nc.vector.tensor_tensor(x1, o_h[:, :, 0:32], ta, ALU.subtract)
                    ins = nc.vector.tensor_tensor(x2, o_h[:, :, 32:64], tb, ALU.add)
                    if m == 0:
                        e.link(ins)
                ins.then_inc(done, e.mark(done, ("rope",)))
                split(u0 + 10)
                for u in (11, 12, 13):
                    split(u0 + u)
                for h in range(4):
                    ins = score(h)
                e.link(ins)
                maxima(0)
                split(u0 + 14)
                for h in range(4, 8):
                    ins = score(h)
                e.link(ins)
                maxima(1)
                split(u0 + 15)
                split(u0 + 16)
                decayed(0, 0)
                split(u0 + 17)
                decayed(0, 1)
                eng.wait_ge(acted, e.after(acted, ("prob", 1)))
                e.link(nc.vector.tensor_tensor(rs[:, :, :], rs[:, :, :], dm[:, :, :], ALU.add))
                e.link(nc.vector.reciprocal(rs[:, :, :], rs[:, :, :]))
                split(u0 + 18)
                weights(0, 0)
                weights(0, 1)
                split(u0 + 19)
                weights(0, 2)
                weights(0, 3)
                split(u0 + 20)
                for b in range(MT):
                    eng.wait_ge(small, e.after(small, ("oa", b)))
                    nc.vector.tensor_tensor(
                        oa[:, b, :].rearrange("p (h d) -> p h d", h=HEADS),
                        bank(("oa", b)).rearrange("p (h d) -> p h d", h=HEADS),
                        rs[:, :, b:b + 1].to_broadcast([P, HEADS, HEAD_DIM]), ALU.mult).then_inc(
                            done, e.mark(done, ("oa", b)))
                decayed(1, 0)
                decayed(1, 1)
                split(u0 + 21)
                for j in range(2):
                    lo_turned(oa_hi, oa_lo, ("oat", j), 2 * j)
                gated(0)
                weights(1, 0)
                weights(1, 1)
                split(u0 + 22)
                split(u0 + 23)
                weights(1, 2)
                weights(1, 3)
                decayed(2, 0)
                split(u0 + 24)
                decayed(2, 1)
                merge("a", 0, 2, u0 + 21)
                gated(1)
                weights(2, 0)
                weights(2, 1)
                split(u0 + 25)
                weights(2, 2)
                weights(2, 3)
                split(u0 + 26)
                merge("a", 1, 0, u0 + 23)
                split(u0 + 27)
                decayed(3, 0)
                decayed(3, 1)
                gated(2)
                for i in range(4):
                    weights(3, i)
                split(u0 + 28)
                gated(3)
                eng.wait_ge(done, e.after(done, ("ob", 3)))
                nc.vector.tensor_scalar(so[:, 1, :], so[:, 0, :], 1.0 / DV, EPS, ALU.mult, ALU.add).then_inc(
                    done, e.mark(done, ("so",)))
                eng.wait_ge(acted, e.after(acted, ("so_root",)))
                e.link(nc.vector.reciprocal(so[:, 2, :], so[:, 2, :]))
                rsqrt_newton(so[:, 3, :], so[:, 1, :], so[:, 2, :], so[:, 4, :], ("rso",))
                for h in range(GLA_HEADS):
                    for m in range(MT):
                        part = rb[:, m, h * DV:(h + 1) * DV]
                        ins = nc.vector.tensor_scalar(part, part, so[:, 3, 2 * h + m:2 * h + m + 1], None, ALU.mult)
                ins.then_inc(done, e.mark(done, ("obn",)))
                split(u0 + 29)
                for j in range(2):
                    lo_turned(ob_hi, ob_lo, ("obt", j), 2 * j, V_OUT_NORM + 2 * j)
                split(u0 + 30)
                for j in (2, 3):
                    lo_turned(ob_hi, ob_lo, ("obt", j), 2 * j, V_OUT_NORM + 2 * j)
                split(u0 + 31)
                split(u0 + 32)
                merge("b", 0, 0, u0 + 29)
                split(u0 + 33)
                for j in range(2):
                    lo_turned(mt2_hi, mt2_lo, ("mt", 0, j), 2 * j)
                split(u0 + 34)
                merge("b", 1, 1, u0 + 31)
                for j in range(2):
                    lo_turned(mt2_hi, mt2_lo, ("mt", 1, j), 4 + 2 * j)
                split(u0 + 35)
                split(u0 + 36)
                multiplied(u0 + 33)
                add_to_x(2, 0, 1.0).then_inc(done, e.mark(done, ("x", "ffn1", 0)))
                x_lo("ffn1", 0)
                split(u0 + 37)

            eng.sem_inc(w_ready, RAW)
            eng.sem_inc(hid_done, 2)
            eng.sem_inc(ht_done, 2)
            for b in (1, 2):
                eng.wait_ge(small, e.after(small, ("vecs", b)))
                at = {1: 0, 2: VR[1]}[b]
                col, per = 0, VR[b] // LAYERS
                for name, rows in VEC_ROWS[b]:
                    src = psum[:, 3 + b, col * LAYERS:(col + rows) * LAYERS].rearrange("p (l r) -> p l r", l=LAYERS)
                    dst = vecs[:, at:at + VR[b]].rearrange("p (l r) -> p l r", l=LAYERS)[:, :, col:col + rows]
                    e.link(nc.vector.tensor_copy(dst, src))
                    col += rows
                if b == 1:
                    small_vectors(0, per)
            nc.vector.tensor_copy(vecs[:, VR[1] + VR[2]:], vecs[:, 0:VR[2] // LAYERS]).then_inc(
                done, e.mark(done, ("vecs",)))
            eng.sem_inc(x_whole, 1)
            x_lo("ffn0", 0)
            half_done()
            for u in range(2):
                split(u)
            eng.wait_ge(done, e.after(done, ("vecs",)))
            with e.layers(1):
                ffn_vector(0, 0, "mix")
                mix1_vector(FFN_UNITS)
                ffn_vector(FFN_UNITS + MIX_UNITS[1], 1, "ffn0")
            e.enter("between")
            norm("final")
            eng.wait_ge(gfin_in, 16)
            for half in range(2):
                cols = slice(512 * half, 512 * half + 512)
                for m in range(MT):
                    ins = nc.vector.scalar_tensor_tensor(out=x[:, m, cols], in0=x[:, m, cols],
                                                         scalar=rstd[:, m:m + 1], in1=gfin[:, cols],
                                                         op0=ALU.mult, op1=ALU.mult)
                if half == 0:
                    ins.then_inc(done, e.mark(done, ("final", 0)))
            ins.then_inc(x_whole, 1)
            x_lo("ffn0", 0)
            half_done()
            with e.layers(2):
                ffn_vector(0, 0, "mix")
                mix2_vector(FFN_UNITS)
                ffn_vector(FFN_UNITS + MIX_UNITS[2], 1, "ffn0")
            e.enter("end")

    return counts


def tables():
    t = np.arange(T)
    angle = 2 * np.pi * ((t[:, None] * t[None, :]) % T) / T
    t_cs = np.concatenate([np.cos(angle), np.sin(angle)], axis=1) / np.sqrt(T)
    c = np.arange(P)
    angle = 2 * np.pi * ((c[:, None] * c[None, :]) % P) / P
    t_cc = np.concatenate([np.cos(angle), -np.sin(angle)], axis=1) / np.sqrt(P)
    pools = []
    for w in (2, 4, 8, 16):
        half = w // 2
        count = np.minimum(t + half, T) - np.maximum(t - half, 0)
        inside = (t[:, None] >= t[None, :] - half) & (t[:, None] < t[None, :] + half)
        pools.append(inside / count[None, :] - np.eye(T))
    out = {"t_ident": np.eye(P), "t_cs": t_cs, "t_cc": t_cc, "t_pool": np.concatenate(pools, axis=1)}
    s, q = np.arange(P)[:, None], np.arange(P)[None, :]
    spans, pairs = [], []
    for lv in range(LEVELS - 1):
        n = 1 << lv
        border = q // (2 * n) * 2 * n + n
        odd = q // n % 2 == 1
        spans.append(np.where(odd, (s >= border) & (s <= q), (s > q) & (s < border)))
        pairs.append((s // (2 * n) == q // (2 * n)) & (s // n % 2 == 0) & odd)
    last = [s > q, s <= q]
    parts = [spans[0:4], spans[4:7] + last[0:1], spans[4:7] + last[1:2]]
    out["t_spans"] = np.concatenate([w for part in parts for w in part], axis=1) / TAU
    out["t_pairs"] = np.concatenate(pairs + [s == q], axis=1)
    query, key = s, q
    out["t_window"] = np.where(np.concatenate([key <= query, key > query, key <= query], axis=1), 0.0, -1e30)
    inv_freq = np.float32(10000.0) ** (-np.arange(0, HEAD_DIM, 2, dtype=np.float32) / np.float32(HEAD_DIM))
    angle = np.arange(T, dtype=np.float32)[:, None] * inv_freq[None, :]
    out["t_rope"] = np.concatenate([np.cos(angle), np.sin(angle)], axis=1)
    return {k: np.ascontiguousarray(w.astype(np.float32)) for k, w in out.items()}


def kernel(**inputs):
    import concourse.bacc as bacc
    from concourse.bass_utils import run_bass_kernel_spmd

    arrays = {k: np.ascontiguousarray(w) for k, w in inputs.items()}
    arrays.update(tables())

    def program(known):
        nc = bacc.Bacc("TRN2", target_bir_lowering=False, num_devices=1)
        a = {k: nc.dram_tensor(k + "_dram", w.shape, F32, kind="ExternalInput").ap() for k, w in arrays.items()}
        a["out"] = nc.dram_tensor("out_dram", (1, T, D), F32, kind="ExternalOutput").ap()
        return nc, build(nc, a, known)

    _, counts = program(None)
    nc, again = program(counts)
    assert again == counts
    result = run_bass_kernel_spmd(nc, [{k + "_dram": w for k, w in arrays.items()}], core_ids=[0])
    return result.results[0]["out_dram"]
```
